# Optimizing a Trainium2 kernel written in Bass

```python
import jax, jax.numpy as jnp
from jax import lax
import numpy as np

D_MODEL = 1024
BATCH = 1
SEQ = 128
DEPTH = 4
DEC_BATCH = 1
DEC_SEQ = 512
PAST_LEN = 128

GRID_W = 64
N_MIXERS = 3
N_CONV_LAYERS = (DEPTH + 2) // 3
N_POOL_LAYERS = (DEPTH + 1) // 3
N_ATTN_LAYERS = DEPTH // 3
N_HEADS = 8
N_KV_HEADS = 2
HEAD_DIM = 128
ROPE_AXIS_DIM = HEAD_DIM // 2
ROPE_THETA = 10000.0
Q_BLOCK = 128
CONV_WIDTH = 3
POOL_WINDOWS = (2, 4, 8, 16)
N_POOL_GROUPS = 4
POOL_GROUP_DIM = D_MODEL // N_POOL_GROUPS
D_FF = ((8 * D_MODEL // 3 + 255) // 256) * 256
N_MOD = 6
EPS = 1e-6
ATTN_SCALE = HEAD_DIM ** -0.5

kernel_name = 'hybrid_flow_prefix_trunk_step'

def rms_norm(x, w):
    xf = x.astype(jnp.float32)
    y = xf * lax.rsqrt(jnp.mean(xf * xf, axis=-1, keepdims=True) + EPS)
    return (y * w.astype(jnp.float32)).astype(x.dtype)

def adaln(c, w, b):
    m = (jax.nn.silu(c) @ w + b).reshape(c.shape[0], N_MOD, 1, D_MODEL)
    return [m[:, i] for i in range(N_MOD)]

def modulate(x, shift, scale):
    return x * (1 + scale) + shift

def short_conv_mixer(h, w_in, conv_w, w_out):
    b, cg, u = jnp.split(h @ w_in, 3, axis=-1)
    z = cg * u
    zp = jnp.pad(z, ((0, 0), (1, 1), (0, 0)))
    conv = zp[:, :-2] * conv_w[0] + zp[:, 1:-1] * conv_w[1] + zp[:, 2:] * conv_w[2]
    return (b * conv) @ w_out

def pool_mixer(h, w_pool, scale):
    B, T, D = h.shape
    hf = h.astype(jnp.float32)
    cs = jnp.concatenate([jnp.zeros((B, 1, D), jnp.float32), jnp.cumsum(hf, axis=1)], axis=1)
    csg = cs.reshape(B, T + 1, N_POOL_GROUPS, POOL_GROUP_DIM)
    t = jnp.arange(T)
    pooled = []
    for g, w in enumerate(POOL_WINDOWS):
        lo = jnp.clip(t - w // 2, 0, T)
        hi = jnp.clip(t + w // 2, 0, T)
        cnt = (hi - lo).astype(jnp.float32)[None, :, None]
        pooled.append((csg[:, hi, g] - csg[:, lo, g]) / cnt)
    pooled = jnp.stack(pooled, axis=2)
    diff = (pooled - hf.reshape(B, T, N_POOL_GROUPS, POOL_GROUP_DIM)).astype(h.dtype)
    out = jnp.einsum('btgc,gcd->btgd', diff, w_pool).reshape(B, T, D)
    return out * scale

def swiglu(h, w_in, w_out):
    g, u = jnp.split(h @ w_in, 2, axis=-1)
    return (jax.nn.silu(g) * u) @ w_out

def qkv_project(h, w_qkv, q_norm_w, k_norm_w):
    B, T, _ = h.shape
    qkv = h @ w_qkv
    q = qkv[..., :N_HEADS * HEAD_DIM].reshape(B, T, N_HEADS, HEAD_DIM)
    k = qkv[..., N_HEADS * HEAD_DIM:(N_HEADS + N_KV_HEADS) * HEAD_DIM].reshape(B, T, N_KV_HEADS, HEAD_DIM)
    v = qkv[..., (N_HEADS + N_KV_HEADS) * HEAD_DIM:].reshape(B, T, N_KV_HEADS, HEAD_DIM)
    q = rms_norm(q, q_norm_w)
    k = rms_norm(k, k_norm_w)
    return (jnp.transpose(q, (0, 2, 1, 3)), jnp.transpose(k, (0, 2, 1, 3)),
            jnp.transpose(v, (0, 2, 1, 3)))

def rope_axis(x, cos, sin):
    x1, x2 = jnp.split(x, 2, axis=-1)
    return jnp.concatenate([x1 * cos - x2 * sin, x2 * cos + x1 * sin], axis=-1)

def apply_rope_2d(x, cos_r, sin_r, cos_c, sin_c):
    xr = rope_axis(x[..., :ROPE_AXIS_DIM], cos_r.astype(x.dtype), sin_r.astype(x.dtype))
    xc = rope_axis(x[..., ROPE_AXIS_DIM:], cos_c.astype(x.dtype), sin_c.astype(x.dtype))
    return jnp.concatenate([xr, xc], axis=-1)

def block_attention(q, k, v):
    B, Hq, T, Dh = q.shape
    Hkv = k.shape[1]
    G = Hq // Hkv
    nb = T // Q_BLOCK
    qb = jnp.moveaxis(q.reshape(B, Hkv, G, nb, Q_BLOCK, Dh), 3, 0)

    def one_block(qblk):
        s = jnp.einsum('bhgqd,bhkd->bhgqk', qblk, k,
                       preferred_element_type=jnp.float32) * ATTN_SCALE
        p = jax.nn.softmax(s, axis=-1).astype(v.dtype)
        return jnp.einsum('bhgqk,bhkd->bhgqd', p, v)

    ob = lax.map(one_block, qb)
    return jnp.moveaxis(ob, 0, 3).reshape(B, Hq, T, Dh)

def merge_heads(o, w_out):
    B, H, T, Dh = o.shape
    return jnp.transpose(o, (0, 2, 1, 3)).reshape(B, T, H * Dh) @ w_out

def setup_inputs(seed: int = 0) -> dict:
    key = jax.random.key(seed)
    ks = jax.random.split(key, 24)
    nrm = jax.random.normal
    f32 = jnp.float32
    D = D_MODEL
    qkv_out = (N_HEADS + 2 * N_KV_HEADS) * HEAD_DIM
    return {
        'x_prompt': nrm(ks[0], (BATCH, SEQ, D), f32),
        'x_sample': nrm(ks[1], (DEC_BATCH, DEC_SEQ, D), f32),
        'cache_k': nrm(ks[2], (DEC_BATCH, N_ATTN_LAYERS, N_KV_HEADS, PAST_LEN, HEAD_DIM), f32),
        'cache_v': nrm(ks[3], (DEC_BATCH, N_ATTN_LAYERS, N_KV_HEADS, PAST_LEN, HEAD_DIM), f32),
        'c': nrm(ks[4], (DEC_BATCH, D), f32),
        'c_ctx': nrm(ks[5], (D,), f32),
        'norm1_w': 1.0 + 0.05 * nrm(ks[6], (DEPTH, D), f32),
        'norm2_w': 1.0 + 0.05 * nrm(ks[7], (DEPTH, D), f32),
        'ada_w': 0.5 * D ** -0.5 * nrm(ks[8], (DEPTH, D, N_MOD * D), f32),
        'ada_b': 0.01 * nrm(ks[9], (DEPTH, N_MOD * D), f32),
        'conv_in_w': D ** -0.5 * nrm(ks[10], (N_CONV_LAYERS, D, 3 * D), f32),
        'conv_w': CONV_WIDTH ** -0.5 * nrm(ks[11], (N_CONV_LAYERS, CONV_WIDTH, D), f32),
        'conv_out_w': D ** -0.5 * nrm(ks[12], (N_CONV_LAYERS, D, D), f32),
        'pool_w': POOL_GROUP_DIM ** -0.5 * nrm(ks[13], (N_POOL_LAYERS, N_POOL_GROUPS, POOL_GROUP_DIM, POOL_GROUP_DIM), f32),
        'pool_scale': 1.0 + 0.1 * nrm(ks[14], (N_POOL_LAYERS, D), f32),
        'attn_qkv_w': D ** -0.5 * nrm(ks[15], (N_ATTN_LAYERS, D, qkv_out), f32),
        'q_norm_w': 1.0 + 0.05 * nrm(ks[16], (N_ATTN_LAYERS, HEAD_DIM), f32),
        'k_norm_w': 1.0 + 0.05 * nrm(ks[17], (N_ATTN_LAYERS, HEAD_DIM), f32),
        'attn_out_w': (N_HEADS * HEAD_DIM) ** -0.5 * nrm(ks[18], (N_ATTN_LAYERS, N_HEADS * HEAD_DIM, D), f32),
        'ffn_in_w': D ** -0.5 * nrm(ks[19], (DEPTH, D, 2 * D_FF), f32),
        'ffn_out_w': D_FF ** -0.5 * nrm(ks[20], (DEPTH, D_FF, D), f32),
        'final_norm_w': 1.0 + 0.05 * nrm(ks[21], (D,), f32),
    }

def reference(x_prompt, x_sample, cache_k, cache_v, c, c_ctx, norm1_w, norm2_w, ada_w, ada_b,
              conv_in_w, conv_w, conv_out_w, pool_w, pool_scale, attn_qkv_w, q_norm_w, k_norm_w,
              attn_out_w, ffn_in_w, ffn_out_w, final_norm_w):
    T = x_sample.shape[1]
    rows = T // GRID_W
    row = jnp.repeat(jnp.arange(rows), GRID_W).astype(jnp.float32)
    col = jnp.tile(jnp.arange(GRID_W), rows).astype(jnp.float32)
    inv_freq = ROPE_THETA ** (-jnp.arange(0, ROPE_AXIS_DIM, 2, dtype=jnp.float32) / ROPE_AXIS_DIM)
    ang_r = row[:, None] * inv_freq[None, :]
    ang_c = col[:, None] * inv_freq[None, :]
    cos_r, sin_r, cos_c, sin_c = jnp.cos(ang_r), jnp.sin(ang_r), jnp.cos(ang_c), jnp.sin(ang_c)

    xp, xs = x_prompt, x_sample
    new_k, new_v = [], []
    for i in range(DEPTH):
        kind = i % N_MIXERS
        j = i // N_MIXERS
        mod_p = adaln(c_ctx[None, :], ada_w[i], ada_b[i])
        mod_s = adaln(c, ada_w[i], ada_b[i])
        hp = modulate(rms_norm(xp, norm1_w[i]), mod_p[0], mod_p[1])
        hs = modulate(rms_norm(xs, norm1_w[i]), mod_s[0], mod_s[1])
        if kind == 0:
            mp = short_conv_mixer(hp, conv_in_w[j], conv_w[j], conv_out_w[j])
            ms = short_conv_mixer(hs, conv_in_w[j], conv_w[j], conv_out_w[j])
        elif kind == 1:
            mp = pool_mixer(hp, pool_w[j], pool_scale[j])
            ms = pool_mixer(hs, pool_w[j], pool_scale[j])
        else:
            qp, kp, vp = qkv_project(hp, attn_qkv_w[j], q_norm_w[j], k_norm_w[j])
            new_k.append(kp)
            new_v.append(vp)
            mp = merge_heads(block_attention(qp, kp, vp), attn_out_w[j])
            qs, ks_, vs = qkv_project(hs, attn_qkv_w[j], q_norm_w[j], k_norm_w[j])
            qs = apply_rope_2d(qs, cos_r, sin_r, cos_c, sin_c)
            ks_ = apply_rope_2d(ks_, cos_r, sin_r, cos_c, sin_c)
            k_all = jnp.concatenate([cache_k[:, j].astype(ks_.dtype), ks_], axis=2)
            v_all = jnp.concatenate([cache_v[:, j].astype(vs.dtype), vs], axis=2)
            ms = merge_heads(block_attention(qs, k_all, v_all), attn_out_w[j])
        xp = xp + mod_p[2] * mp
        xs = xs + mod_s[2] * ms
        hp = modulate(rms_norm(xp, norm2_w[i]), mod_p[3], mod_p[4])
        hs = modulate(rms_norm(xs, norm2_w[i]), mod_s[3], mod_s[4])
        xp = xp + mod_p[5] * swiglu(hp, ffn_in_w[i], ffn_out_w[i])
        xs = xs + mod_s[5] * swiglu(hs, ffn_in_w[i], ffn_out_w[i])

    y_prompt = rms_norm(xp, final_norm_w)
    y_sample = rms_norm(xs, final_norm_w)
    new_k_arr = jnp.stack(new_k, axis=1)
    new_v_arr = jnp.stack(new_v, axis=1)
    return (y_prompt, y_sample, new_k_arr, new_v_arr)


_drawn_inputs = setup_inputs


def setup_inputs(seed=0):
    import zlib

    import numpy as np

    out = dict(_drawn_inputs(seed))
    spreads = {}
    factors = {'cache_k': 8.0, 'cache_v': 6.706, 'q_norm_w': 8.0}
    for name, (base, spread) in spreads.items():
        noise = np.random.default_rng([zlib.crc32(name.encode()), seed]).standard_normal(out[name].shape)
        drawn = base * np.exp(spread * noise) if base else spread * noise
        out[name] = __import__('jax').numpy.asarray(drawn.astype(out[name].dtype))
    for name, factor in factors.items():
        out[name] = (out[name] * factor).astype(out[name].dtype)
    return out
```

```python
from contextlib import ExitStack

import concourse.bass as bass
import numpy as np
from concourse import mybir

F32 = mybir.dt.float32
F32R = mybir.dt.float32r
ALU = mybir.AluOpType
ACT = mybir.ActivationFunctionType
AX = mybir.AxisListType

P = 128
D = 1024
KD = D // P
DEPTH = 4
TS = 512
TP = 128
T = TS + TP
DFF = 2816
FT = DFF // P
CHUNK = 8
LAST = FT - 2 * CHUNK
HEADS = 8
KVH = 2
GRID_W = 64
EPS = 1e-6
SCALE = float(P) ** -0.5
WINDOWS = (2, 4, 8, 16)
NMOD = 6
TA = 256
Q_ZU, Q_B, Q_OUT, Q_QKV, Q_IN, Q_LAST = 4, 2, 2, 3, 4, LAST // 2
Q_FFN = 2 * (Q_IN + Q_OUT) + Q_LAST + Q_OUT
KIND = [("conv", "pool", "attn")[i % 3] for i in range(DEPTH)]
Q_MIX = {"conv": Q_ZU + Q_B + Q_OUT, "pool": Q_OUT, "attn": Q_QKV + Q_OUT}
LAYER_Q = [sum(Q_MIX[KIND[n]] + Q_FFN for n in range(i)) for i in range(DEPTH + 1)]
QUADS = LAYER_Q[DEPTH]
ADA_T = NMOD * KD
ADA_Q = ADA_T // 4
ADA_HEAD = 4
G_MIX = {"conv": KD, "pool": KD, "attn": HEADS}
LAYER_G = [sum(G_MIX[KIND[n]] + FT for n in range(i)) for i in range(DEPTH + 1)]
SHIFT1, SCALE1, GATE1, SHIFT2, SCALE2, GATE2 = range(6)
H_BASE = [KD * (n - sum(KIND[m // 2] == "pool" and m % 2 == 0 for m in range(n))) for n in range(2 * DEPTH)]
CS, CP, CW = 1, TS + 3, T + 4
HP = 8
PS0, PP0, PW = HP, TS + 3 * HP, T + 4 * HP


def build(nc, d):
    with ExitStack() as ctx:
        def sb(name, shape, dt=F32):
            return ctx.enter_context(nc.sbuf_tensor(name, shape, dt))

        def sem(name):
            return ctx.enter_context(nc.semaphore(name))

        x = sb("x", [P, KD, T])
        h_hi = sb("h_hi", [P, KD, T], F32R)
        h_lo = sb("h_lo", [P, KD, T], F32R)
        g_hi = sb("g_hi", [P, CHUNK, T], F32R)
        g_lo = sb("g_lo", [P, CHUNK, T], F32R)
        raw = sb("raw", [P, 4, KD * P])
        w_hi = sb("w_hi", [P, 2, KD * P], F32R)
        w_lo = sb("w_lo", [P, 2, KD * P], F32R)
        ada_w = sb("ada_w", [P, 4, KD * P])
        mix = sb("mix", [P, 12 * T])
        tmp = sb("tmp", [P, 6, PW])
        rope = sb("rope", [P, 2, TS])
        cache_k = sb("cache_k", [P, KVH, P])
        cache_v = sb("cache_v", [P, KVH, P])
        ones = sb("ones", [P, P])
        ident = sb("ident", [P, P])
        turn = sb("turn", [P, P])
        mod = sb("mod", [P, DEPTH * ADA_T, 2])
        ada_b = sb("ada_b", [P, DEPTH * ADA_T, 2])
        norm_w = sb("norm_w", [P, DEPTH * 2 * KD, 2])
        gain = sb("gain", [P, DEPTH * 2 * KD, 2])
        pool_gate = sb("pool_gate", [P, KD, 2])
        pool_s = sb("pool_s", [P, KD, 2])
        cond = sb("cond", [P, KD, 2])
        cond_s = sb("cond_s", [P, KD, 2])
        conv_w = sb("conv_w", [P, 2 * 3 * KD])
        qk_norm = sb("qk_norm", [P, 2])
        final_w = sb("final_w", [P, KD])
        edge = sb("edge", [P, len(WINDOWS), 4 * HP])
        eps = sb("eps", [P, 1])
        stat = sb("stat", [P, 4, 2])
        marks = sb("marks", [P, 4])

        ps = ctx.enter_context(nc.psum_tensor("ps", [P, 4, 512], F32))
        ps_ada = ctx.enter_context(nc.psum_tensor("ps_ada", [P, 512], F32))
        ps_sum = ctx.enter_context(nc.psum_tensor("ps_sum", [P, 2, 512], F32))
        ps_rot = ctx.enter_context(nc.psum_tensor("ps_rot", [P, 512], F32))
        sum_flat = ps_sum[:].rearrange("p b n -> p (b n)")
        ps_flat = [ps[:, 2 * s:2 * s + 2, :].rearrange("p b n -> p (b n)") for s in range(2)]
        prob_t = ada_w[:].rearrange("p a n -> p (a n)")
        prob_s = prob_t[:, 0:5 * TS].rearrange("p (k q) -> p k q", k=5)
        prob_p = prob_t[:, 5 * TS:5 * TS + TP]
        v_tok = prob_t[:, 5 * TS + TP:5 * TS + TP + KVH * T].rearrange("p (h t) -> p h t", h=KVH)
        sq, sq_sum, rms, rinv = tmp[:, 0:2, 0:T], tmp[:, 2, 0:T], tmp[:, 3, 0:T], tmp[:, 3, 0:T]
        head_root = tmp[:, 5, 0:T]
        pair_a, pair_b = tmp[:, 0:2, 0:T], tmp[:, 4:6, 0:T]

        consts_in = sem("consts_in")
        x_in = sem("x_in")
        raw_in = [sem(f"raw_in{j}") for j in range(4)]
        ada_in = [sem(f"ada_in{j}") for j in range(4)]
        w_hi_ready = sem("w_hi_ready")
        w_lo_ready = sem("w_lo_ready")
        unit_done = sem("unit_done")
        freed = [sem("even_freed"), sem("odd_freed")]
        ada_done = sem("ada_done")
        ada_kept = sem("ada_kept")
        cond_ready = sem("cond_ready")
        gain_ready = sem("gain_ready")
        ones_ready = sem("ones_ready")
        sq_ready = sem("sq_ready")
        sq_added = sem("sq_added")
        sum_ready = sem("sum_ready")
        rms_ready = sem("rms_ready")
        rinv_ready = sem("rinv_ready")
        scaled = sem("scaled")
        h_hi_ready = sem("h_hi_ready")
        h_ready = sem("h_ready")
        g_hi_ready = sem("g_hi_ready")
        g_ready = sem("g_ready")
        pads_ready = sem("pads_ready")
        conv_step = sem("conv_step")
        pool_step = sem("pool_step")
        diff_ready = sem("diff_ready")
        head_step = sem("head_step")
        v_turned = sem("v_turned")
        v_kept = sem("v_kept")
        head_sq = sem("head_sq")
        head_sum = sem("head_sum")
        head_rms = sem("head_rms")
        head_normed = sem("head_normed")
        head_turned = sem("head_turned")
        head_ready = sem("head_ready")
        q_held = sem("q_held")
        score_done = sem("score_done")
        max_done = sem("max_done")
        bias_done = sem("bias_done")
        exp_done = sem("exp_done")
        inv_done = sem("inv_done")
        prob_ready = sem("prob_ready")
        prob_turned = sem("prob_turned")
        prob_kept = sem("prob_kept")
        mixed_done = sem("mixed_done")
        kv_stored = sem("kv_stored")
        y_ready = sem("y_ready")
        y_stored = sem("y_stored")

        block = ctx.enter_context(nc.Block())

        def sample_of(slot):
            return ps[:, 2 * slot:2 * slot + 2, 0:TA]

        def prompt_of(slot):
            return ps[:, 2 * slot + 1, TA:TA + TP]

        def halves(row):
            return row.rearrange("p (b n) -> p b n", b=2)

        def parts(slot, row, off_s=0, off_p=TS):
            return ((sample_of(slot), halves(row[:, off_s:off_s + TS])),
                    (prompt_of(slot), row[:, off_p:off_p + TP]))

        def k_of(layer, phase):
            return {"pool": 2, "last": LAST}.get(phase, KD)

        @block.sync
        def _(sp):
            for dst, name in ((cond, "cond"), (ada_b, "ada_b"), (norm_w, "norm_w"), (ident, "ident"),
                              (turn, "turn"), (conv_w, "conv_w"), (qk_norm, "qk_norm"),
                              (final_w, "final_w"), (edge, "edge"), (pool_s, "pool_s"),
                              (rope, "rope"), (cache_k, "cache_k"), (cache_v, "cache_v")):
                sp.dma_start(dst[:], d[name]).then_inc(consts_in, 16)

            def load(q, tiles, first=False):
                for j in range(4):
                    if not first:
                        sp.wait_ge(w_lo_ready, 4 * q + (j - 3))
                    sp.dma_start(raw[:, j, 0:tiles * P], d["weights"][4 * q + j, :, 0:tiles * P]).then_inc(raw_in[j], 16)

            def load_ada(qa, j, first=False):
                if not first:
                    sp.wait_ge(ada_done, 4 * qa + (j - 3))
                sp.dma_start(ada_w[:, j, :], d["ada_w"][4 * qa + j]).then_inc(ada_in[j], 16)

            def load_both(q, tiles, qa):
                for j in range(4):
                    sp.wait_ge(w_lo_ready, 4 * q + (j - 3))
                    sp.dma_start(raw[:, j, 0:tiles * P], d["weights"][4 * q + j, :, 0:tiles * P]).then_inc(raw_in[j], 16)
                    load_ada(qa, j)

            for j in range(4):
                load_ada(0, j, first=True)
            sp.dma_start(x[:], d["x"]).then_inc(x_in, 16)
            load(0, KD, first=True)
            with sp.Fori(1, ADA_HEAD) as i:
                for j in range(4):
                    load_ada(i, j)
            for layer in range(DEPTH):
                q = LAYER_Q[layer]
                kind = KIND[layer]
                qa = ADA_Q * (layer + 1)
                if layer == 0:
                    for j in range(4):
                        load_ada(ADA_HEAD, j)
                    with sp.Fori(1, Q_MIX["conv"]) as i:
                        load_both(i, KD, i + ADA_HEAD)
                elif kind == "pool":
                    load(q, 2)
                    load(q + 1, 2)
                else:
                    with sp.Fori(0, Q_MIX[kind]) as i:
                        load(i + q, KD)
                if kind == "attn":
                    sp.wait_ge(head_ready, KVH)
                    sp.dma_start(d["new_v"], mix[:, 0:2 * T].rearrange("p (h t) -> p h t", h=KVH)[:, :, TS:T]).then_inc(kv_stored, 16)
                    sp.dma_start(d["new_k"], mix[:, 2 * T:4 * T].rearrange("p (h t) -> p h t", h=KVH)[:, :, TS:T]).then_inc(kv_stored, 16)
                    sp.wait_ge(mixed_done, HEADS)
                q += Q_MIX[kind]
                if layer + 1 < DEPTH:
                    with sp.Fori(0, 2 * (Q_IN + Q_OUT)) as i:
                        load_both(i + q, KD, i + qa)
                else:
                    with sp.Fori(0, 2 * (Q_IN + Q_OUT)) as i:
                        load(i + q, KD)
                q += 2 * (Q_IN + Q_OUT)
                with sp.Fori(0, Q_LAST) as i:
                    load(i + q, KD)
                q += Q_LAST
                with sp.Fori(0, Q_OUT) as i:
                    load(i + q, LAST)
            for k in range(KD):
                sp.wait_ge(y_ready, k + 1)
                sp.dma_start(d["y"][:, k, :], mix[:, k * T:(k + 1) * T]).then_inc(y_stored, 16)
            sp.wait_ge(kv_stored, 32)
            sp.wait_ge(y_stored, 16 * KD)

        @block.gpsimd
        def _(pool):
            pool.memset(ones[:], 1.0).then_inc(ones_ready, 1)
            pool.memset(eps[:], EPS).then_inc(ones_ready, 1)
            for n, free in enumerate(freed):
                pool.memset(marks[:, n:n + 1], 0.0).then_inc(free, 1)

            def hold(h, s):
                pool.wait_ge(head_ready, h + (KVH + 1))
                pool.tensor_copy(tmp[:, 2 + s, 0:T], mix[:, bass.ds(h * T + 4 * T, T)]).then_inc(q_held, 1)

            hold(0, 0)
            hold(1, 1)
            with pool.Fori(1, HEADS // 2) as i:
                for s in range(2):
                    pool.wait_ge(score_done, 10 * i + (5 * s - 5))
                    hold(2 * i + s, s)

        @block.tensor
        def _(pe):
            def products(q, j, a_hi, a_lo, tiles, ready=None):
                slot = j % 2
                pe.wait_ge(w_lo_ready, 4 * q + (j + 1))
                pe.wait_ge(freed[slot], 2 * q + (j // 2 + 1))
                for k in range(tiles):
                    if ready is not None:
                        pe.wait_ge(ready[0], ready[1] + k + 1)
                    ws = slice(k * P, k * P + P)
                    passes = ((w_hi, a_hi), (w_hi, a_lo), (w_lo, a_hi))
                    for n, (w, a) in enumerate(passes):
                        begin, end = k == 0 and n == 0, k == tiles - 1 and n == 2
                        pe.matmul(ps[:, 2 * slot, 0:TA], w[:, slot, ws], a(k)[:, 0:TA], start=begin, stop=end)
                        mm = pe.matmul(ps[:, 2 * slot + 1, 0:T - TA], w[:, slot, ws], a(k)[:, TA:T], start=begin, stop=end)
                mm.then_inc(unit_done, 1)

            def h_quad(q, n, ada=None):
                for j in range(4):
                    products(q, j, lambda k: h_hi[:, k, :], lambda k: h_lo[:, k, :], KD,
                             ready=(h_ready, H_BASE[n]) if j == 0 else None)
                    if ada is not None:
                        ada_products(ada, j)

            def g_quad(q, tiles, base, ada=None):
                for j in range(4):
                    products(q, j, lambda k: g_hi[:, k, :], lambda k: g_lo[:, k, :], tiles,
                             ready=(g_ready, base) if j == 0 else None)
                    if ada is not None:
                        ada_products(ada, j)

            def ada_products(qa, j, first=False):
                pe.wait_ge(ada_in[j], 16 * qa + 16)
                if j == 0 and not first:
                    pe.wait_ge(ada_kept, qa)
                for k in range(KD):
                    mm = pe.matmul(ps_ada[:, 2 * j:2 * j + 2], ada_w[:, j, k * P:k * P + P], cond_s[:, k, :],
                                   start=(k == 0), stop=(k == KD - 1))
                mm.then_inc(ada_done, 1)

            def sum_features(src, s, value, done):
                pe.wait_ge(s, value)
                pe.matmul(ps_sum[:, 0, 0:TA], ones[:], src[:, 0:TA], start=True, stop=True)
                pe.matmul(ps_sum[:, 1, 0:T - TA], ones[:], src[:, TA:T], start=True, stop=True).then_inc(done, 1)

            def attention():
                def turn_v(v):
                    pe.wait_ge(freed[v], 2 * LAYER_Q[layer] + 2)
                    if v:
                        pe.wait_ge(v_kept, v)
                    for k in range(T // P):
                        mm = pe.transpose(sum_flat[:, k * P:(k + 1) * P], mix[:, v * T + k * P:v * T + (k + 1) * P], ident[:])
                    mm.then_inc(v_turned, 1)

                def head_sums(t):
                    if t == KVH:
                        pe.wait_ge(v_kept, KVH)
                    else:
                        pe.wait_ge(head_rms, t - KVH)
                    sum_features(tmp[:, t % 2, 0:T], head_sq, t - 1, head_sum)

                def head_turn(t):
                    pe.wait_ge(head_normed, t - 1)
                    if t > KVH:
                        pe.wait_ge(head_ready, t - KVH)
                    pe.matmul(ps_rot[:], turn[:], mix[:, t * T:t * T + TS], start=True, stop=True).then_inc(head_turned, 1)

                q0 = LAYER_Q[layer]
                for t in range(4 * Q_QKV + 2):
                    if t < 4 * Q_QKV:
                        products(q0 + t // 4, t % 4, lambda k: h_hi[:, k, :], lambda k: h_lo[:, k, :], KD,
                                 ready=(h_ready, H_BASE[2 * layer]) if t == 0 else None)
                    if 1 <= t <= KVH:
                        turn_v(t - 1)
                    if KVH <= t - 1 < 4 * Q_QKV:
                        head_sums(t - 1)
                    if t - 2 >= KVH:
                        head_turn(t - 2)

                def scores(kv, base, n):
                    qt, row = n % 5, tmp[:, 2 + n // 5, :]
                    out = ps_flat[n % 2]
                    if qt == 0:
                        pe.wait_ge(q_held, 2 * base + (n // 5 + 1))
                    if n >= 2:
                        pe.wait_ge(exp_done, 10 * base + (n - 1))
                    key = mix[:, (2 + kv) * T:(3 + kv) * T]
                    if qt < 4:
                        pe.matmul(out[:, 0:TS], row[:, qt * P:(qt + 1) * P], key[:, 0:TS], start=True, stop=True)
                        pe.matmul(out[:, TS:T], row[:, qt * P:(qt + 1) * P], cache_k[:, kv, :], start=True, stop=True).then_inc(score_done, 1)
                    else:
                        pe.matmul(out[:, 0:TP], row[:, TS:T], key[:, TS:T], start=True, stop=True).then_inc(score_done, 1)

                def turn_probs(base, n):
                    pe.wait_ge(prob_ready, 10 * base + (n + 1))
                    if n >= 1:
                        pe.wait_ge(prob_kept, 10 * base + n)
                    for k in range(5 if n % 5 < 4 else 1):
                        mm = pe.transpose(sum_flat[:, k * P:(k + 1) * P], tmp[:, n % 2, k * P:(k + 1) * P], ident[:])
                    mm.then_inc(prob_turned, 1)

                def mix_values(kv, base, hh):
                    pe.wait_ge(prob_kept, 10 * base + (5 * hh + 5))
                    pe.wait_ge(g_ready, 2 * base + (LAYER_G[layer] + hh))
                    for k in range(5):
                        val = v_tok[:, kv, k * P:(k + 1) * P] if k < 4 else cache_v[:, kv, :]
                        pe.matmul(ps_rot[:], val, prob_s[:, k, :], start=(k == 0), stop=(k == 4))
                    pe.matmul(ps_ada[:, 0:TP], v_tok[:, kv, TS:T], prob_p, start=True, stop=True).then_inc(mixed_done, 1)

                for kv in range(KVH):
                    with pe.Fori(2 * kv, 2 * kv + 2) as i:
                        scores(kv, i, 0)
                        scores(kv, i, 1)
                        for n in range(10):
                            if n + 2 < 10:
                                scores(kv, i, n + 2)
                            if n == 5:
                                mix_values(kv, i, 0)
                            turn_probs(i, n)
                        mix_values(kv, i, 1)

            pe.wait_ge(cond_ready, 1)
            for j in range(4):
                ada_products(0, j, first=True)
            with pe.Fori(1, ADA_HEAD) as i:
                for j in range(4):
                    ada_products(i, j)
            pe.wait_ge(consts_in, 13 * 16)
            pe.wait_ge(ones_ready, 2)
            for layer in range(DEPTH):
                q, g, kind = LAYER_Q[layer], LAYER_G[layer], KIND[layer]
                sum_features(sq_sum, sq_added, (KD - 1) * (2 * layer + 1), sum_ready)
                if kind == "conv":
                    with pe.Fori(0, Q_ZU + Q_B) as i:
                        h_quad(i + q, 2 * layer, ada=i + ADA_HEAD if layer == 0 else None)
                    with pe.Fori(0, Q_OUT) as i:
                        g_quad(i + (q + Q_ZU + Q_B), KD, g, ada=i + (ADA_HEAD + Q_ZU + Q_B) if layer == 0 else None)
                elif kind == "pool":
                    for m in range(KD):
                        pair = m // 2 * 2
                        products(q + m // 4, m % 4, lambda k: g_hi[:, pair + k, :], lambda k: g_lo[:, pair + k, :], 2,
                                 ready=(g_ready, g + pair))
                else:
                    attention()
                    with pe.Fori(0, Q_OUT) as i:
                        g_quad(i + (q + Q_QKV), KD, g)
                q += Q_MIX[kind]
                g += G_MIX[kind]
                sum_features(sq_sum, sq_added, (KD - 1) * (2 * layer + 2), sum_ready)
                qa = ADA_Q * (layer + 1)
                ada = layer + 1 < DEPTH
                with pe.Fori(0, 2) as c:
                    with pe.Fori(0, Q_IN) as i:
                        h_quad(c * (Q_IN + Q_OUT) + i + q, 2 * layer + 1,
                               ada=c * (Q_IN + Q_OUT) + i + qa if ada else None)
                    with pe.Fori(0, Q_OUT) as i:
                        g_quad(c * (Q_IN + Q_OUT) + i + (q + Q_IN), CHUNK, c * CHUNK + g,
                               ada=c * (Q_IN + Q_OUT) + i + (qa + Q_IN) if ada else None)
                q += 2 * (Q_IN + Q_OUT)
                with pe.Fori(0, Q_LAST) as i:
                    h_quad(i + q, 2 * layer + 1)
                with pe.Fori(0, Q_OUT) as i:
                    g_quad(i + (q + Q_LAST), LAST, g + 2 * CHUNK)
            sum_features(sq_sum, sq_added, (KD - 1) * (2 * DEPTH + 1), sum_ready)

        @block.scalar
        def _(act):
            def split_hi(q, j, tiles):
                act.wait_ge(raw_in[j], 16 * q + 16)
                act.activation(w_hi[:, j % 2, 0:tiles * P], raw[:, j, 0:tiles * P], ACT.Copy).then_inc(w_hi_ready, 1)

            def step(q, j, tiles):
                act.wait_ge(unit_done, 4 * q + (j + 1))
                if tiles:
                    split_hi(q + (j + 2) // 4, (j + 2) % 4, tiles)

            def evacuated(q, j):
                return 2 * q + (j // 2 + 2)

            def g_hi_of(src, index):
                act.activation(g_hi[:, index, :], src, ACT.Copy).then_inc(g_hi_ready, 1)

            def ffn_in_quad(q, i, tiles=(KD,) * 4):
                for j in range(4):
                    step(q, j, tiles[j])
                    if j % 2 == 0:
                        for src, dst in parts(0, pair_a[:, j // 2, :]):
                            a = act.activation(dst, src, ACT.Silu)
                        a.then_inc(freed[0], 1)
                    else:
                        act.wait_ge(freed[1], evacuated(q, j))
                        g_hi_of(pair_b[:, j // 2, :], bass.ds(2 * i + j // 2, 1) if not isinstance(i, int) else slice(2 * i + j // 2, 2 * i + j // 2 + 1))

            def out_quad(q, m0, n, tiles, squares):
                for j in range(4):
                    step(q, j, tiles[j])
                    if squares:
                        m = m0 + j
                        act.wait_ge(freed[j % 2], evacuated(q, j))
                        square(m, n)

            def square(m, n):
                if m >= 3:
                    act.wait_ge(sq_added, (KD - 1) * n + m - 2)
                act.activation(sq[:, m % 2, :] if m else sq_sum, x[:, m, :], ACT.Square).then_inc(sq_ready, 1)

            def rms_of(n):
                act.wait_ge(sum_ready, n + 1)
                act.activation(rms[:, 0:TA], ps_sum[:, 0, 0:TA], ACT.Sqrt, bias=eps[:], scale=1.0 / D)
                act.activation(rms[:, TA:T], ps_sum[:, 1, 0:T - TA], ACT.Sqrt, bias=eps[:], scale=1.0 / D).then_inc(rms_ready, 1)

            def normed(layer, which, padded=False):
                n = 2 * layer + which
                rms_of(n)
                shift = ADA_T * layer + KD * (SHIFT1, SHIFT2)[which]
                with act.Fori(0, KD // 2) as i:
                    for s in range(2):
                        act.wait_ge(scaled, 2 * i + (KD * n + s + 1))
                        for g, lo, hi in ((0, 0, TS), (1, TS, T)):
                            if padded:
                                at = (PS0, PP0)[g]
                                dst = mix[:, bass.ds(i * (2 * PW) + (s * PW + at), hi - lo)]
                            else:
                                dst = h_hi[:, bass.ds(2 * i + s, 1), lo:hi]
                            src = pair_b[:, s:s + 1, lo:hi] if not padded else pair_b[:, s, lo:hi]
                            a = act.activation(dst, src, ACT.Identity,
                                               bias=mod[:, bass.ds(2 * i + (shift + s), 1), g:g + 1].rearrange("p a b -> p (a b)"))
                        a.then_inc(h_hi_ready, 1)

            def attention(q0):
                for t in range(4 * Q_QKV + 1):
                    if t < 4 * Q_QKV:
                        step(q0 + t // 4, t % 4, KD)
                        for src, dst in parts(t % 2, mix[:, t * T:(t + 1) * T]):
                            a = act.activation(dst, src, ACT.Copy)
                        a.then_inc(freed[t % 2], 1)
                    if KVH <= t - 1:
                        act.wait_ge(head_sum, t - KVH)
                        if t - 1 > KVH:
                            act.wait_ge(head_normed, t - 1 - KVH)
                        act.activation(head_root[:, 0:TA], ps_sum[:, 0, 0:TA], ACT.Sqrt, bias=eps[:], scale=1.0 / P)
                        act.activation(head_root[:, TA:T], ps_sum[:, 1, 0:T - TA], ACT.Sqrt, bias=eps[:], scale=1.0 / P).then_inc(head_rms, 1)
                    if KVH <= t < 4 * Q_QKV:
                        act.wait_ge(freed[t % 2], evacuated(q0 + t // 4, t % 4))
                        act.activation(tmp[:, t % 2, 0:T], mix[:, t * T:(t + 1) * T], ACT.Square).then_inc(head_sq, 1)

                def softmax_exp(i, n):
                    width = T if n % 5 < 4 else TP
                    act.wait_ge(bias_done, 10 * i + (n + 1))
                    act.activation(tmp[:, n % 2, 0:width], ps_flat[n % 2][:, 0:width], ACT.Exp,
                                   bias=stat[:, 1, n % 2:n % 2 + 1], scale=SCALE,
                                   accum_out=stat[:, 2, n % 2:n % 2 + 1]).then_inc(exp_done, 1)

                def keep_probs(i, n):
                    act.wait_ge(prob_turned, 10 * i + (n + 1))
                    if n == 5:
                        act.wait_ge(mixed_done, 2 * i + 1)
                    if n % 5 < 4:
                        dst = prob_s[:, :, (n % 5) * P:(n % 5 + 1) * P]
                        src = sum_flat[:, 0:T].rearrange("p (k q) -> p k q", k=5)
                    else:
                        dst, src = prob_p, sum_flat[:, 0:P]
                    act.activation(dst, src, ACT.Copy).then_inc(prob_kept, 1)

                def mixed_hi(i, hh):
                    act.wait_ge(mixed_done, 2 * i + (hh + 1))
                    act.activation(g_hi[:, bass.ds(2 * i + hh, 1), 0:TS], ps_rot[:].rearrange("p (a n) -> p a n", a=1), ACT.Copy)
                    act.activation(g_hi[:, bass.ds(2 * i + hh, 1), TS:T], ps_ada[:, 0:TP].rearrange("p (a n) -> p a n", a=1), ACT.Copy).then_inc(g_hi_ready, 1)

                with act.Fori(0, HEADS // 2) as i:
                    softmax_exp(i, 0)
                    for n in range(10):
                        if n + 1 < 10:
                            softmax_exp(i, n + 1)
                        if n == 5:
                            mixed_hi(i, 0)
                        keep_probs(i, n)
                    mixed_hi(i, 1)

            act.wait_ge(consts_in, 13 * 16)
            act.wait_ge(ones_ready, 2)
            act.activation(cond_s[:], cond[:], ACT.Silu).then_inc(cond_ready, 1)
            act.wait_ge(x_in, 16)
            for m in range(KD):
                square(m, 0)
            split_hi(0, 0, KD)
            split_hi(0, 1, KD)
            for layer in range(DEPTH):
                q, g, kind = LAYER_Q[layer], LAYER_G[layer], KIND[layer]
                normed(layer, 0, padded=(kind == "pool"))
                if kind == "conv":
                    with act.Fori(0, Q_ZU) as i:
                        for j in range(4):
                            step(i + q, j, KD)
                            if j % 2 == 0:
                                for src, dst in parts(0, pair_a[:, j // 2, :]):
                                    a = act.activation(dst, src, ACT.Copy)
                                a.then_inc(freed[0], 1)
                    q += Q_ZU
                    with act.Fori(0, Q_B) as i:
                        for j in range(4):
                            step(i + q, j, KD)
                            act.wait_ge(freed[j % 2], evacuated(i + q, j))
                            g_hi_of(pair_b[:, j % 2:j % 2 + 1, :], bass.ds(4 * i + j, 1))
                    q += Q_B
                elif kind == "pool":
                    for k in range(KD):
                        act.wait_ge(diff_ready, k + 1)
                        act.activation(g_hi[:, k, :], pair_b[:, k % 2, :], ACT.Copy).then_inc(g_hi_ready, 1)
                else:
                    attention(q)
                    q += Q_QKV
                last_pair = (2 if kind == "pool" else KD,) * 2 + (KD,) * 2
                out_quad(q, 0, 2 * layer + 1, (2,) * 4 if kind == "pool" else (KD,) * 4, True)
                out_quad(q + 1, 4, 2 * layer + 1, last_pair, True)
                q += Q_OUT
                normed(layer, 1)
                with act.Fori(0, 2) as c:
                    with act.Fori(0, Q_IN) as i:
                        ffn_in_quad(c * (Q_IN + Q_OUT) + i + q, i)
                    with act.Fori(0, Q_OUT) as i:
                        out_quad(c * (Q_IN + Q_OUT) + i + (q + Q_IN), 0, 0, (KD,) * 4, False)
                q += 2 * (Q_IN + Q_OUT)
                with act.Fori(0, Q_LAST - 1) as i:
                    ffn_in_quad(i + q, i)
                q += Q_LAST - 1
                ffn_in_quad(q, Q_LAST - 1, (KD, KD, LAST, LAST))
                q += 1
                after = 0 if layer + 1 == DEPTH else 2 if KIND[layer + 1] == "pool" else KD
                out_quad(q, 0, 2 * layer + 2, (LAST,) * 4, True)
                out_quad(q + 1, 4, 2 * layer + 2, (LAST, LAST, after, after), True)
            rms_of(2 * DEPTH)

        @block.vector
        def _(dve):
            def split_lo(q, j, tiles):
                dve.wait_ge(w_hi_ready, 4 * q + (j + 1))
                dve.tensor_tensor(w_lo[:, j % 2, 0:tiles * P], raw[:, j, 0:tiles * P],
                                  w_hi[:, j % 2, 0:tiles * P].bitcast(F32), ALU.subtract).then_inc(w_lo_ready, 1)

            def step(q, j, tiles):
                if tiles:
                    split_lo(q + (j + 2) // 4, (j + 2) % 4, tiles)
                dve.wait_ge(unit_done, 4 * q + (j + 1))

            def evacuated(q, j):
                return 2 * q + (j // 2 + 2)

            def g_lo_of(src, index, count):
                dve.wait_ge(g_hi_ready, count)
                dve.tensor_tensor(g_lo[:, index, :], src, g_hi[:, index, :].bitcast(F32), ALU.subtract).then_inc(g_ready, 1)
                dve.wait_ge(g_ready, count)

            def keep_ada(qa):
                dve.wait_ge(ada_done, 4 * qa + 4)
                dve.tensor_tensor(mod[:, bass.ds(4 * qa, 4), :], ps_ada[:, 0:8].rearrange("p (a b) -> p a b", a=4),
                                  ada_b[:, bass.ds(4 * qa, 4), :], ALU.add).then_inc(ada_kept, 1)

            def gain_of(layer, which):
                dve.wait_ge(ada_kept, (ADA_HEAD if layer == 0 and which == 0 else ADA_Q * (layer + 1)))
                at = ADA_T * layer + KD * (SCALE1, SCALE2)[which]
                o = KD * (2 * layer + which)
                dve.scalar_tensor_tensor(out=gain[:, o:o + KD, :], in0=mod[:, at:at + KD, :], scalar=1.0,
                                         in1=norm_w[:, o:o + KD, :], op0=ALU.add, op1=ALU.mult).then_inc(gain_ready, 1)

            def ffn_in_quad(q, i, count, ada=None, tiles=(KD,) * 4):
                for j in range(4):
                    step(q, j, tiles[j])
                    if j % 2:
                        pair = j // 2
                        dve.wait_ge(freed[0], evacuated(q, j))
                        for (src, dst), (_, gate) in zip(parts(1, pair_b[:, pair, :]), parts(1, pair_a[:, pair, :])):
                            v = dve.tensor_tensor(dst, src, gate, ALU.mult)
                        v.then_inc(freed[1], 1)
                        index = slice(2 * i + pair, 2 * i + pair + 1) if isinstance(i, int) else bass.ds(2 * i + pair, 1)
                        g_lo_of(pair_b[:, pair:pair + 1, :], index, count + (pair + 1))
                if ada is not None:
                    keep_ada(ada)

            def out_quad(q, m0, n, gate, tiles, squares, ada=None):
                for j in range(4):
                    step(q, j, tiles[j])
                    for g, (src, dst) in enumerate(parts(j % 2, x[:, m0 + j, :]) if isinstance(m0, int) else
                                                   dynamic_parts(j % 2, m0 + j)):
                        v = dve.scalar_tensor_tensor(out=dst, in0=src, scalar=gate(m0 + j, g), in1=dst,
                                                     op0=ALU.mult, op1=ALU.add)
                    v.then_inc(freed[j % 2], 1)
                    if squares and m0 + j >= 2:
                        add_square(m0 + j - 1, n)
                if squares and m0:
                    add_square(KD - 1, n)
                if ada is not None:
                    keep_ada(ada)

            def dynamic_parts(slot, m):
                row = x[:, bass.ds(m, 1), :].rearrange("p a t -> p (a t)")
                return parts(slot, row)

            def add_square(m, n):
                dve.wait_ge(sq_ready, KD * n + m + 1)
                if m >= 2:
                    dve.wait_ge(sq_added, (KD - 1) * n + m - 1)
                dve.tensor_tensor(sq_sum, sq_sum, sq[:, m % 2, :], ALU.add).then_inc(sq_added, 1)

            def gate_of(block_):
                def gate(m, g):
                    at = ADA_T * layer + KD * block_
                    if isinstance(m, int):
                        return mod[:, at + m, g:g + 1]
                    return mod[:, bass.ds(m + at, 1), g:g + 1].rearrange("p a b -> p (a b)")
                return gate

            def inverse_rms(n):
                dve.wait_ge(rms_ready, n + 1)
                dve.reciprocal(rinv, rms).then_inc(rinv_ready, 1)
                dve.wait_ge(rinv_ready, n + 1)

            def normed(layer, which, padded=False):
                n = 2 * layer + which
                shift = ADA_T * layer + KD * (SHIFT1, SHIFT2)[which]
                inverse_rms(n)
                dve.wait_ge(gain_ready, n + 1)
                with dve.Fori(0, KD // 2) as i:
                    for s in range(2):
                        for g, lo, hi in ((0, 0, TS), (1, TS, T)):
                            v = dve.scalar_tensor_tensor(
                                out=pair_b[:, s:s + 1, lo:hi], in0=x[:, bass.ds(2 * i + s, 1), lo:hi],
                                scalar=gain[:, bass.ds(2 * i + (KD * n + s), 1), g:g + 1].rearrange("p a b -> p (a b)"),
                                in1=tmp[:, 3:4, lo:hi], op0=ALU.mult, op1=ALU.mult)
                        v.then_inc(scaled, 1)
                    for s in range(2):
                        dve.wait_ge(h_hi_ready, 2 * i + (KD * n + s + 1))
                        if padded:
                            continue
                        for g, lo, hi in ((0, 0, TS), (1, TS, T)):
                            v = dve.scalar_tensor_tensor(
                                out=h_lo[:, bass.ds(2 * i + s, 1), lo:hi], in0=pair_b[:, s:s + 1, lo:hi],
                                scalar=mod[:, bass.ds(2 * i + (shift + s), 1), g:g + 1].rearrange("p a b -> p (a b)"),
                                in1=h_hi[:, bass.ds(2 * i + s, 1), lo:hi].bitcast(F32), op0=ALU.add, op1=ALU.subtract)
                        v.then_inc(h_ready, 1)
                    if not padded:
                        dve.wait_ge(h_ready, 2 * i + (H_BASE[n] + 2))

            def conv(layer, q, g):
                ada = layer == 0
                jc = layer // 3
                z = tmp[:, 4:6, 0:CW]
                for at in (0, CS + TS, CP - 1, CW - 1):
                    dve.memset(z[:, :, at:at + 1], 0.0)
                dve.memset(marks[:, 3:4], 0.0).then_inc(pads_ready, 1)
                dve.wait_ge(pads_ready, jc + 1 + (1 if layer > 1 else 0))
                if layer:
                    dve.wait_ge(kv_stored, 32)
                with dve.Fori(0, Q_ZU) as i:
                    for j in range(4):
                        step(i + q, j, KD)
                        if j % 2:
                            pair = j // 2
                            dve.wait_ge(freed[0], evacuated(i + q, j))
                            row = z[:, pair, :]
                            for (src, dst), (_, c) in zip(parts(1, row, CS, CP), parts(1, pair_a[:, pair, :])):
                                v = dve.tensor_tensor(dst, src, c, ALU.mult)
                            v.then_inc(freed[1], 1)
                            dve.wait_ge(freed[1], evacuated(i + q, j))
                            out = mix[:, bass.ds(i * (2 * CW) + (pair * CW + 1), CW - 2)]
                            for n, tap in enumerate((1, 0, 2)):
                                w = conv_w[:, bass.ds(2 * i + ((jc * 3 + tap) * KD + pair), 1)]
                                if n == 0:
                                    v = dve.tensor_scalar(out, row[:, 1:CW - 1], w, None, ALU.mult)
                                else:
                                    dve.wait_ge(conv_step, 6 * i + (jc * 3 * KD + 3 * pair + n))
                                    v = dve.scalar_tensor_tensor(out=out, in0=row[:, tap:tap + CW - 2], scalar=w,
                                                                 in1=out, op0=ALU.mult, op1=ALU.add)
                                v.then_inc(conv_step, 1)
                            dve.wait_ge(conv_step, 6 * i + (jc * 3 * KD + 3 * pair + 3))
                    if ada:
                        keep_ada(i + ADA_HEAD)
                q += Q_ZU
                dve.wait_ge(conv_step, (jc + 1) * 3 * KD)
                with dve.Fori(0, Q_B) as i:
                    for j in range(4):
                        step(i + q, j, KD)
                        row = mix[:, bass.ds(i * (4 * CW) + j * CW, CW)]
                        for (src, dst), (_, c) in zip(parts(j % 2, pair_b[:, j % 2, :]), parts(j % 2, row, CS, CP)):
                            v = dve.tensor_tensor(dst, src, c, ALU.mult)
                        v.then_inc(freed[j % 2], 1)
                        g_lo_of(pair_b[:, j % 2:j % 2 + 1, :], bass.ds(4 * i + j, 1), 4 * i + (g + j + 1))
                    if ada:
                        keep_ada(i + (ADA_HEAD + Q_ZU))
                q += Q_B
                for half in range(Q_OUT):
                    out_quad(q + half, 4 * half, 2 * layer + 1, gate_of(GATE1), (KD,) * 4, True,
                             ada=ADA_HEAD + Q_ZU + Q_B + half if ada else None)

            def pooling(layer, q, g):
                steps = [0]

                def chained(ins):
                    ins.then_inc(pool_step, 1)
                    steps[0] += 1
                    dve.wait_ge(pool_step, steps[0])

                normed(layer, 0, padded=True)
                chained(dve.tensor_tensor(pool_gate[:], pool_s[:], mod[:, ADA_T * layer + KD * GATE1:ADA_T * layer + KD * (GATE1 + 1), :], ALU.mult))
                for k in range(KD):
                    h = mix[:, k * PW:(k + 1) * PW]
                    src, a, b = h, tmp[:, 0, :], tmp[:, 1, :]
                    group = k // (KD // len(WINDOWS))
                    w = WINDOWS[group]
                    half, lo, hi = 1, 1, PW
                    chained(dve.tensor_tensor(a[:, lo:hi], src[:, lo - 1:hi - 1], src[:, lo:hi], ALU.add))
                    src = a
                    other = b
                    size = 2
                    while size < w:
                        s = size // 2
                        lo, hi = lo + s, hi - s
                        chained(dve.tensor_tensor(other[:, lo:hi], src[:, lo - s:hi - s], src[:, lo + s:hi + s], ALU.add))
                        src, other = other, src
                        size *= 2
                    for n, (at, length) in enumerate(((PS0, TS), (PP0, TP))):
                        for e, o in enumerate((at, at + length - HP)):
                            v = dve.tensor_tensor(src[:, o:o + HP], src[:, o:o + HP],
                                                  edge[:, group, (2 * n + e) * HP:(2 * n + e + 1) * HP], ALU.mult)
                    chained(v)
                    for at, lo_, n_ in ((PS0, 0, TS), (PP0, TS, TP)):
                        v = dve.scalar_tensor_tensor(out=pair_b[:, k % 2, lo_:lo_ + n_], in0=src[:, at:at + n_], scalar=1.0 / w,
                                                     in1=h[:, at:at + n_], op0=ALU.mult, op1=ALU.subtract)
                    v.then_inc(diff_ready, 1)
                    g_lo_of(pair_b[:, k % 2, :], k, g + k + 1)
                pg = lambda m, g_: pool_gate[:, m, g_:g_ + 1]
                out_quad(q, 0, 2 * layer + 1, pg, (2,) * 4, True)
                out_quad(q + 1, 4, 2 * layer + 1, pg, (2, 2, KD, KD), True)

            def attention(layer, q, g):
                steps = [0]

                def chained(ins):
                    ins.then_inc(head_step, 1)
                    steps[0] += 1
                    dve.wait_ge(head_step, steps[0])

                for t in range(4 * Q_QKV + 2):
                    if t < 4 * Q_QKV:
                        step(q + t // 4, t % 4, KD)
                    if 1 <= t <= KVH:
                        dve.wait_ge(v_turned, t)
                        dve.tensor_copy(v_tok[:, t - 1, :], sum_flat[:, 0:T]).then_inc(v_kept, 1)
                    if t - 2 >= KVH:
                        row = mix[:, (t - 2) * T:(t - 2) * T + TS]
                        dve.wait_ge(head_turned, t - 3)
                        dve.tensor_tensor(tmp[:, 4, 0:TS], ps_rot[:], rope[:, 1, :], ALU.mult)
                        chained(dve.tensor_tensor(row, row, rope[:, 0, :], ALU.mult))
                        dve.tensor_tensor(row, row, tmp[:, 4, 0:TS], ALU.add).then_inc(head_ready, 1)
                        dve.wait_ge(head_ready, t - 3)
                    if KVH <= t - 1 < 4 * Q_QKV:
                        row = mix[:, (t - 1) * T:t * T]
                        dve.wait_ge(head_rms, t - KVH)
                        chained(dve.reciprocal(head_root, head_root))
                        w = qk_norm[:, 1:2] if t - 1 < 2 * KVH else qk_norm[:, 0:1]
                        dve.scalar_tensor_tensor(out=row, in0=row, scalar=w, in1=head_root,
                                                 op0=ALU.mult, op1=ALU.mult).then_inc(head_normed, 1)

                def row_max(i, n):
                    width = T if n % 5 < 4 else TP
                    dve.wait_ge(score_done, 10 * i + (n + 1))
                    dve.tensor_reduce(stat[:, 0, n % 2:n % 2 + 1], ps_flat[n % 2][:, 0:width], AX.X, ALU.max).then_inc(max_done, 1)
                    dve.wait_ge(max_done, 10 * i + (n + 1))
                    dve.tensor_scalar(stat[:, 1, n % 2:n % 2 + 1], stat[:, 0, n % 2:n % 2 + 1], -SCALE, None, ALU.mult).then_inc(bias_done, 1)

                def normalise(i, n):
                    width = T if n % 5 < 4 else TP
                    dve.wait_ge(exp_done, 10 * i + (n + 1))
                    dve.reciprocal(stat[:, 3, n % 2:n % 2 + 1], stat[:, 2, n % 2:n % 2 + 1]).then_inc(inv_done, 1)
                    dve.wait_ge(inv_done, 10 * i + (n + 1))
                    dve.tensor_scalar(tmp[:, n % 2, 0:width], tmp[:, n % 2, 0:width], stat[:, 3, n % 2:n % 2 + 1],
                                      None, ALU.mult).then_inc(prob_ready, 1)

                def mixed_lo(i, hh):
                    dve.wait_ge(g_hi_ready, 2 * i + (g + hh + 1))
                    at = bass.ds(2 * i + hh, 1)
                    dve.tensor_tensor(g_lo[:, at, 0:TS], ps_rot[:].rearrange("p (a n) -> p a n", a=1),
                                      g_hi[:, at, 0:TS].bitcast(F32), ALU.subtract)
                    dve.tensor_tensor(g_lo[:, at, TS:T], ps_ada[:, 0:TP].rearrange("p (a n) -> p a n", a=1),
                                      g_hi[:, at, TS:T].bitcast(F32), ALU.subtract).then_inc(g_ready, 1)

                with dve.Fori(0, HEADS // 2) as i:
                    row_max(i, 0)
                    for n in range(10):
                        if n + 1 < 10:
                            row_max(i, n + 1)
                        normalise(i, n)
                        if n == 7:
                            mixed_lo(i, 0)
                    mixed_lo(i, 1)
                q += Q_QKV
                for half in range(Q_OUT):
                    out_quad(q + half, 4 * half, 2 * layer + 1, gate_of(GATE1), (KD,) * 4, True)

            dve.wait_ge(consts_in, 13 * 16)
            dve.wait_ge(x_in, 16)
            for m in range(1, KD):
                add_square(m, 0)
            split_lo(0, 0, KD)
            split_lo(0, 1, KD)
            with dve.Fori(0, ADA_HEAD) as i:
                keep_ada(i)
            gain_of(0, 0)
            for layer in range(DEPTH):
                q, g, kind = LAYER_Q[layer], LAYER_G[layer], KIND[layer]
                if kind == "pool":
                    for o in range(KD):
                        for a, b in ((0, PS0), (PS0 + TS, PP0), (PP0 + TP, PW)):
                            dve.memset(mix[:, o * PW + a:o * PW + b], 0.0)
                    dve.memset(marks[:, 3:4], 0.0).then_inc(pads_ready, 1)
                    dve.wait_ge(pads_ready, 2)
                    pooling(layer, q, g)
                else:
                    normed(layer, 0)
                    (conv if kind == "conv" else attention)(layer, q, g)
                if layer == 0:
                    gain_of(0, 1)
                q += Q_MIX[kind]
                g += G_MIX[kind]
                normed(layer, 1)
                ada = layer + 1 < DEPTH
                qa = ADA_Q * (layer + 1)
                with dve.Fori(0, 2) as c:
                    with dve.Fori(0, Q_IN) as i:
                        ffn_in_quad(c * (Q_IN + Q_OUT) + i + q, i, c * CHUNK + 2 * i + g,
                                    ada=c * (Q_IN + Q_OUT) + i + qa if ada else None)
                    with dve.Fori(0, Q_OUT) as i:
                        out_quad(c * (Q_IN + Q_OUT) + i + (q + Q_IN), 4 * i, 0, gate_of(GATE2), (KD,) * 4, False,
                                 ada=c * (Q_IN + Q_OUT) + i + (qa + Q_IN) if ada else None)
                if ada:
                    gain_of(layer + 1, 0)
                    gain_of(layer + 1, 1)
                q += 2 * (Q_IN + Q_OUT)
                g += 2 * CHUNK
                with dve.Fori(0, Q_LAST - 1) as i:
                    ffn_in_quad(i + q, i, 2 * i + g)
                q += Q_LAST - 1
                ffn_in_quad(q, Q_LAST - 1, g + 2 * (Q_LAST - 1), tiles=(KD, KD, LAST, LAST))
                q += 1
                after = 0 if layer + 1 == DEPTH else 2 if KIND[layer + 1] == "pool" else KD
                out_quad(q, 0, 2 * layer + 2, gate_of(GATE2), (LAST,) * 4, True)
                out_quad(q + 1, 4, 2 * layer + 2, gate_of(GATE2), (LAST, LAST, after, after), True)
            inverse_rms(2 * DEPTH)
            for k in range(KD):
                dve.scalar_tensor_tensor(out=mix[:, k * T:(k + 1) * T], in0=x[:, k, :], scalar=final_w[:, k:k + 1],
                                         in1=rinv, op0=ALU.mult, op1=ALU.mult).then_inc(y_ready, 1)


def _units(w, order):
    k, n = w.shape
    u = w.reshape(k // P, P, n // P, P).transpose(2, 1, 0, 3)[order].reshape(len(order), P, k)
    if k < KD * P:
        u = np.concatenate([u, np.zeros((len(order), P, KD * P - k), w.dtype)], axis=2)
    return u


def _rows(v):
    return np.moveaxis(v.reshape(*v.shape[:-1], -1, P), -1, 0)


def _twice(v):
    return np.repeat(v[..., None], 2, axis=-1)


def _rope():
    axis = P // 2
    inv = 10000.0 ** (-np.arange(0, axis, 2, dtype=np.float32) / np.float32(axis))
    t = np.arange(TS)
    out = np.zeros((P, 2, TS), np.float32)
    for a, pos in enumerate((t // GRID_W, t % GRID_W)):
        ang = (pos[None, :].astype(np.float32) * inv[:, None].astype(np.float32)).astype(np.float32)
        for half in range(2):
            at = a * axis + half * (axis // 2)
            out[at:at + axis // 2, 0] = np.cos(ang)
            out[at:at + axis // 2, 1] = np.sin(ang)
    return out


def _turn():
    m = np.zeros((P, P), np.float32)
    for a in range(0, P, 64):
        for i in range(32):
            m[a + 32 + i, a + i] = -1.0
            m[a + i, a + 32 + i] = 1.0
    return m


def _edge():
    out = np.ones((P, len(WINDOWS), 4 * HP), np.float32)
    for g, w in enumerate(WINDOWS):
        for n, length in enumerate((TS, TP)):
            for e, start in enumerate((0, length - HP)):
                for i in range(HP):
                    t = start + i
                    count = min(t + w // 2, length) - max(t - w // 2, 0)
                    out[:, g, (2 * n + e) * HP + i] = w / count
    return out


def kernel(**inputs):
    import concourse.bacc as _bacc
    from concourse.bass_utils import run_bass_kernel_spmd as _run

    a = {k: np.asarray(v) for k, v in inputs.items()}
    ffn_in = [np.concatenate([_units(a["ffn_in_w"][i], [n for j in range(FT) for n in (j, FT + j)])]) for i in range(DEPTH)]

    def ffn(i):
        w_out = a["ffn_out_w"][i]
        parts_ = []
        for c in range(3):
            lo, hi = CHUNK * c, min(CHUNK * (c + 1), FT)
            parts_.append(ffn_in[i][2 * lo:2 * hi])
            parts_.append(_units(w_out[lo * P:hi * P], list(range(KD))))
        return parts_

    units = []
    for i in range(DEPTH):
        j = i // 3
        if KIND[i] == "conv":
            units.append(_units(a["conv_in_w"][j], [n for m in range(KD) for n in (KD + m, 2 * KD + m)] + list(range(KD))))
            units.append(_units(a["conv_out_w"][j], list(range(KD))))
        elif KIND[i] == "pool":
            units += [_units(a["pool_w"][j, g], [0, 1]) for g in range(len(WINDOWS))]
        else:
            units.append(_units(a["attn_qkv_w"][j], [10, 11, 8, 9, *range(HEADS)]))
            units.append(_units(a["attn_out_w"][j], list(range(KD))))
        units += ffn(i)
    tokens = np.concatenate([a["x_sample"][0], a["x_prompt"][0]], axis=0)
    arrays = {
        "weights": np.concatenate(units),
        "ada_w": np.concatenate([_units(a["ada_w"][i], list(range(ADA_T))) for i in range(DEPTH)]),
        "x": _rows(tokens).transpose(0, 2, 1),
        "cond": np.stack([_rows(a["c"][0]), _rows(a["c_ctx"])], axis=-1),
        "ada_b": _twice(_rows(a["ada_b"]).reshape(P, -1)),
        "norm_w": _twice(_rows(np.stack([a["norm1_w"], a["norm2_w"]], axis=1)).reshape(P, -1)),
        "ident": np.eye(P, dtype=np.float32),
        "turn": _turn(),
        "conv_w": _rows(a["conv_w"]).reshape(P, -1),
        "qk_norm": np.stack([a["q_norm_w"][0], a["k_norm_w"][0]], axis=-1),
        "final_w": _rows(a["final_norm_w"]),
        "edge": _edge(),
        "pool_s": _twice(_rows(a["pool_scale"][0])),
        "rope": _rope(),
        "cache_k": a["cache_k"][0, 0].transpose(2, 0, 1),
        "cache_v": a["cache_v"][0, 0].transpose(1, 0, 2),
    }
    outs = {"y": (P, KD, T), "new_k": (P, KVH, TP), "new_v": (P, KVH, TP)}
    nc = _bacc.Bacc("TRN2", target_bir_lowering=False, num_devices=1)
    d, feed = {}, {}
    for name, v in arrays.items():
        v = np.ascontiguousarray(v)
        feed["in_" + name] = v
        d[name] = nc.dram_tensor("in_" + name, v.shape, mybir.dt.from_np(v.dtype), kind="ExternalInput").ap()
    for name, shape in outs.items():
        d[name] = nc.dram_tensor("out_" + name, shape, F32, kind="ExternalOutput").ap()
    build(nc, d)
    r = _run(nc, [feed], core_ids=[0]).results[0]
    y = r["out_y"].transpose(2, 1, 0).reshape(T, D)
    new_k = r["out_new_k"].transpose(1, 2, 0)[None, None]
    new_v = r["out_new_v"].transpose(1, 2, 0)[None, None]
    return (np.ascontiguousarray(y[TS:][None]), np.ascontiguousarray(y[:TS][None]),
            np.ascontiguousarray(new_k), np.ascontiguousarray(new_v))
```

```python
from contextlib import ExitStack

import concourse.bass as bass
import numpy as np
from concourse import mybir

F32 = mybir.dt.float32
F32R = mybir.dt.float32r
ALU = mybir.AluOpType
ACT = mybir.ActivationFunctionType
AX = mybir.AxisListType

P = 128
D = 1024
KD = D // P
DEPTH = 4
TS = 512
TP = 128
T = TS + TP
DFF = 2816
FT = DFF // P
CHUNK = 8
LAST = FT - 2 * CHUNK
HEADS = 8
KVH = 2
GRID_W = 64
EPS = 1e-6
SCALE = float(P) ** -0.5
WINDOWS = (2, 4, 8, 16)
NMOD = 6
TA = 256
Q_ZU, Q_B, Q_OUT, Q_QKV, Q_IN, Q_LAST = 4, 2, 2, 3, 4, LAST // 2
Q_FFN = 2 * (Q_IN + Q_OUT) + Q_LAST + Q_OUT
KIND = [("conv", "pool", "attn")[i % 3] for i in range(DEPTH)]
Q_MIX = {"conv": Q_ZU + Q_B + Q_OUT, "pool": Q_OUT, "attn": Q_QKV + Q_OUT}
LAYER_Q = [sum(Q_MIX[KIND[n]] + Q_FFN for n in range(i)) for i in range(DEPTH + 1)]
QUADS = LAYER_Q[DEPTH]
ADA_T = NMOD * KD
ADA_N = 3
ADA_Q = ADA_T // ADA_N
ADA_HEAD = -(-2 * KD // ADA_N)
G_MIX = {"conv": KD, "pool": KD, "attn": HEADS}
LAYER_G = [sum(G_MIX[KIND[n]] + FT for n in range(i)) for i in range(DEPTH + 1)]
SHIFT1, SCALE1, GATE1, SHIFT2, SCALE2, GATE2 = range(6)
H_BASE = [KD * (n - sum(KIND[m // 2] == "pool" and m % 2 == 0 for m in range(n))) for n in range(2 * DEPTH)]
CONSTS = 12
CS, CP, CW = 1, TS + 3, T + 4
HP = 8
PS0, PP0, PW = HP, TS + 3 * HP, T + 4 * HP


def build(nc, d):
    with ExitStack() as ctx:
        def sb(name, shape, dt=F32):
            return ctx.enter_context(nc.sbuf_tensor(name, shape, dt))

        def sem(name):
            return ctx.enter_context(nc.semaphore(name))

        x = sb("x", [P, KD, T])
        h_hi = sb("h_hi", [P, KD, T], F32R)
        h_lo = sb("h_lo", [P, KD, T], F32R)
        g_hi = sb("g_hi", [P, CHUNK, T], F32R)
        g_lo = sb("g_lo", [P, CHUNK, T], F32R)
        raw = sb("raw", [P, 4, KD * P])
        w_hi = sb("w_hi", [P, 2, KD * P], F32R)
        w_lo = sb("w_lo", [P, 2, KD * P], F32R)
        ada_w = sb("ada_w", [P, ADA_N * D])
        mix = sb("mix", [P, 12 * T])
        tmp = sb("tmp", [P, 6, PW])
        rope = sb("rope", [P, 2, TS])
        cache_v = sb("cache_v", [P, KVH, P])
        ones = sb("ones", [P, P])
        ident = sb("ident", [P, P])
        turn = sb("turn", [P, P])
        mod = sb("mod", [P, DEPTH * ADA_T, 2])
        gain = sb("gain", [P, DEPTH * 2 * KD, 2])
        pool_gate = sb("pool_gate", [P, KD, 2])
        pool_s = sb("pool_s", [P, KD, 2])
        cond = sb("cond", [P, 2, D])
        ada_raw = sb("ada_raw", [P, ADA_N, 2])
        conv_w = sb("conv_w", [P, 2 * 3 * KD])
        qk_norm = sb("qk_norm", [P, 2])
        final_w = sb("final_w", [P, KD])
        edge = sb("edge", [P, len(WINDOWS), 4 * HP])
        eps = sb("eps", [P, 1])
        stat = sb("stat", [P, 4, 2])
        marks = sb("marks", [P, 4])

        ps = ctx.enter_context(nc.psum_tensor("ps", [P, 4, 512], F32))
        ps_x = ctx.enter_context(nc.psum_tensor("ps_x", [P, 2, 512], F32))
        ps_sum = ctx.enter_context(nc.psum_tensor("ps_sum", [P, 2, 512], F32))
        ps_rot, ps_mixed = ps_x[:, 0, :], ps_x[:, 1, 0:TP]
        ada_products = ps_x[:].rearrange("p b n -> p (b n)")
        sum_flat = ps_sum[:].rearrange("p b n -> p (b n)")
        ps_flat = [ps[:, 2 * s:2 * s + 2, :].rearrange("p b n -> p (b n)") for s in range(2)]
        prob_t = ada_w[:]
        prob_s = prob_t[:, 0:5 * TS].rearrange("p (k q) -> p k q", k=5)
        prob_p = prob_t[:, 5 * TS:5 * TS + TP]
        cache_k = prob_t[:, 5 * TS + TP:5 * TS + TP + KVH * P].rearrange("p (h k) -> p h k", h=KVH)
        v_tok = tmp[:, 4:6, 0:T]
        sq, sq_sum, rms, rinv = tmp[:, 0:2, 0:T], tmp[:, 2, 0:T], tmp[:, 3, 0:T], tmp[:, 3, 0:T]
        head_root = tmp[:, 5, 0:T]
        pair_a, pair_b = tmp[:, 0:2, 0:T], tmp[:, 4:6, 0:T]

        consts_in = sem("consts_in")
        cache_in = sem("cache_in")
        x_in = sem("x_in")
        raw_in = [sem(f"raw_in{j}") for j in range(4)]
        ada_in = [sem(f"ada_in{j}") for j in range(ADA_N)]
        w_hi_ready = sem("w_hi_ready")
        w_lo_ready = sem("w_lo_ready")
        unit_done = sem("unit_done")
        freed = [sem("even_freed"), sem("odd_freed")]
        ada_step = sem("ada_step")
        ada_kept = sem("ada_kept")
        cond_ready = sem("cond_ready")
        gain_ready = sem("gain_ready")
        ones_ready = sem("ones_ready")
        sq_ready = sem("sq_ready")
        sq_added = sem("sq_added")
        sum_ready = sem("sum_ready")
        rms_ready = sem("rms_ready")
        rinv_ready = sem("rinv_ready")
        scaled = sem("scaled")
        h_hi_ready = sem("h_hi_ready")
        h_ready = sem("h_ready")
        g_hi_ready = sem("g_hi_ready")
        g_ready = sem("g_ready")
        pads_ready = sem("pads_ready")
        conv_step = sem("conv_step")
        pool_step = sem("pool_step")
        diff_ready = sem("diff_ready")
        head_step = sem("head_step")
        v_turned = sem("v_turned")
        v_kept = sem("v_kept")
        head_sq = sem("head_sq")
        head_sum = sem("head_sum")
        head_rms = sem("head_rms")
        head_normed = sem("head_normed")
        head_turned = sem("head_turned")
        head_ready = sem("head_ready")
        q_held = sem("q_held")
        score_done = sem("score_done")
        max_done = sem("max_done")
        bias_done = sem("bias_done")
        exp_done = sem("exp_done")
        inv_done = sem("inv_done")
        prob_ready = sem("prob_ready")
        prob_turned = sem("prob_turned")
        prob_kept = sem("prob_kept")
        mixed_done = sem("mixed_done")
        kv_stored = sem("kv_stored")
        y_ready = sem("y_ready")
        y_stored = sem("y_stored")

        block = ctx.enter_context(nc.Block())

        def sample_of(slot):
            return ps[:, 2 * slot:2 * slot + 2, 0:TA]

        def prompt_of(slot):
            return ps[:, 2 * slot + 1, TA:TA + TP]

        def halves(row):
            return row.rearrange("p (b n) -> p b n", b=2)

        def parts(slot, row, off_s=0, off_p=TS):
            return ((sample_of(slot), halves(row[:, off_s:off_s + TS])),
                    (prompt_of(slot), row[:, off_p:off_p + TP]))

        def k_of(layer, phase):
            return {"pool": 2, "last": LAST}.get(phase, KD)

        @block.sync
        def _(sp):
            for dst, name in ((cond, "cond"), (mod, "ada_b"), (gain, "norm_w"), (ident, "ident"),
                              (turn, "turn"), (conv_w, "conv_w"), (qk_norm, "qk_norm"),
                              (final_w, "final_w"), (edge, "edge"), (pool_s, "pool_s"),
                              (rope, "rope"), (cache_v, "cache_v")):
                sp.dma_start(dst[:], d[name]).then_inc(consts_in, 16)

            def load(q, tiles, first=False):
                for j in range(4):
                    if not first:
                        sp.wait_ge(w_lo_ready, 4 * q + (j - 3))
                    sp.dma_start(raw[:, j, 0:tiles * P], d["weights"][4 * q + j, :, 0:tiles * P]).then_inc(raw_in[j], 16)

            def load_ada(qa, j, first=False):
                if not first:
                    sp.wait_ge(ada_step, 2 * ADA_N * qa + (2 * j + 2 - 2 * ADA_N))
                sp.dma_start(ada_w[:, j * D:(j + 1) * D], d["ada_w"][ADA_N * qa + j]).then_inc(ada_in[j], 16)

            def load_both(q, tiles, qa):
                for j in range(4):
                    sp.wait_ge(w_lo_ready, 4 * q + (j - 3))
                    sp.dma_start(raw[:, j, 0:tiles * P], d["weights"][4 * q + j, :, 0:tiles * P]).then_inc(raw_in[j], 16)
                    if j < ADA_N:
                        load_ada(qa, j)

            for j in range(ADA_N):
                load_ada(0, j, first=True)
            sp.dma_start(x[:], d["x"]).then_inc(x_in, 16)
            load(0, KD, first=True)
            with sp.Fori(1, ADA_HEAD) as i:
                for j in range(ADA_N):
                    load_ada(i, j)
            for layer in range(DEPTH):
                q = LAYER_Q[layer]
                kind = KIND[layer]
                qa = ADA_Q * (layer + 1)
                if layer == 0:
                    for j in range(ADA_N):
                        load_ada(ADA_HEAD, j)
                    with sp.Fori(1, Q_ZU + Q_B) as i:
                        load_both(i, KD, i + ADA_HEAD)
                    load_both(Q_ZU + Q_B, KD, ADA_HEAD + Q_ZU + Q_B)
                    load(Q_ZU + Q_B + 1, KD)
                    for n in (1, 2):
                        for j in range(ADA_N):
                            load_ada(ADA_HEAD + Q_ZU + Q_B + n, j)
                    load(Q_MIX["conv"], KD)
                    for n in (3, 4):
                        for j in range(ADA_N):
                            load_ada(ADA_HEAD + Q_ZU + Q_B + n, j)
                elif kind == "pool":
                    load(q, 2)
                    load(q + 1, 2)
                else:
                    if kind == "attn":
                        sp.wait_ge(ada_step, 2 * ADA_N * ADA_Q * (layer + 1))
                        sp.dma_start(cache_k, d["cache_k"]).then_inc(cache_in, 16)
                    with sp.Fori(0, Q_MIX[kind]) as i:
                        load(i + q, KD)
                if kind == "attn":
                    sp.wait_ge(head_ready, KVH)
                    sp.dma_start(d["new_v"], mix[:, 0:2 * T].rearrange("p (h t) -> p h t", h=KVH)[:, :, TS:T]).then_inc(kv_stored, 16)
                    sp.dma_start(d["new_k"], mix[:, 2 * T:4 * T].rearrange("p (h t) -> p h t", h=KVH)[:, :, TS:T]).then_inc(kv_stored, 16)
                    sp.wait_ge(mixed_done, HEADS)
                q += Q_MIX[kind]
                if layer + 1 < DEPTH:
                    with sp.Fori(0 if layer else 1, 2 * (Q_IN + Q_OUT)) as i:
                        load_both(i + q, KD, i + qa)
                else:
                    with sp.Fori(0, 2 * (Q_IN + Q_OUT)) as i:
                        load(i + q, KD)
                q += 2 * (Q_IN + Q_OUT)
                qa += 2 * (Q_IN + Q_OUT)
                more = layer + 1 < DEPTH
                with sp.Fori(0, Q_LAST) as i:
                    if more:
                        load_both(i + q, KD, i + qa)
                    else:
                        load(i + q, KD)
                q += Q_LAST
                if more:
                    load_both(q, LAST, qa + Q_LAST)
                else:
                    load(q, LAST)
                load(q + 1, LAST)
            for k in range(KD):
                sp.wait_ge(y_ready, k + 1)
                sp.dma_start(d["y"][:, k, :], mix[:, k * T:(k + 1) * T]).then_inc(y_stored, 16)
            sp.wait_ge(kv_stored, 32)
            sp.wait_ge(y_stored, 16 * KD)

        @block.gpsimd
        def _(pool):
            pool.memset(ones[:], 1.0).then_inc(ones_ready, 1)
            pool.memset(eps[:], EPS).then_inc(ones_ready, 1)
            for n, free in enumerate(freed):
                pool.memset(marks[:, n:n + 1], 0.0).then_inc(free, 1)

            def hold(h, s):
                pool.wait_ge(head_ready, h + (KVH + 1))
                pool.tensor_copy(tmp[:, 2 + s, 0:T], mix[:, bass.ds(h * T + 4 * T, T)]).then_inc(q_held, 1)

            hold(0, 0)
            hold(1, 1)
            with pool.Fori(1, HEADS // 2) as i:
                for s in range(2):
                    pool.wait_ge(score_done, 10 * i + (5 * s - 5))
                    hold(2 * i + s, s)

        @block.tensor
        def _(pe):
            def products(q, j, a_hi, a_lo, tiles, ready=None):
                slot = j % 2
                pe.wait_ge(w_lo_ready, 4 * q + (j + 1))
                pe.wait_ge(freed[slot], 2 * q + (j // 2 + 1))
                for k in range(tiles):
                    if ready is not None:
                        pe.wait_ge(ready[0], ready[1] + k + 1)
                    ws = slice(k * P, k * P + P)
                    passes = ((w_hi, a_hi), (w_hi, a_lo), (w_lo, a_hi))
                    for n, (w, a) in enumerate(passes):
                        begin, end = k == 0 and n == 0, k == tiles - 1 and n == 2
                        pe.matmul(ps[:, 2 * slot, 0:TA], w[:, slot, ws], a(k)[:, 0:TA], start=begin, stop=end)
                        mm = pe.matmul(ps[:, 2 * slot + 1, 0:T - TA], w[:, slot, ws], a(k)[:, TA:T], start=begin, stop=end)
                mm.then_inc(unit_done, 1)

            def h_quad(q, n):
                for j in range(4):
                    products(q, j, lambda k: h_hi[:, k, :], lambda k: h_lo[:, k, :], KD,
                             ready=(h_ready, H_BASE[n]) if j == 0 else None)

            def g_quad(q, tiles, base):
                for j in range(4):
                    products(q, j, lambda k: g_hi[:, k, :], lambda k: g_lo[:, k, :], tiles,
                             ready=(g_ready, base) if j == 0 else None)

            def sum_features(src, s, value, done):
                pe.wait_ge(s, value)
                pe.matmul(ps_sum[:, 0, 0:TA], ones[:], src[:, 0:TA], start=True, stop=True)
                pe.matmul(ps_sum[:, 1, 0:T - TA], ones[:], src[:, TA:T], start=True, stop=True).then_inc(done, 1)

            def attention():
                def turn_v(v):
                    pe.wait_ge(head_normed, HEADS + KVH)
                    if v:
                        pe.wait_ge(v_kept, v)
                    for k in range(T // P):
                        mm = pe.transpose(sum_flat[:, k * P:(k + 1) * P], mix[:, v * T + k * P:v * T + (k + 1) * P], ident[:])
                    mm.then_inc(v_turned, 1)

                def head_sums(t):
                    if t > KVH:
                        pe.wait_ge(head_rms, t - KVH)
                    sum_features(tmp[:, t % 2, 0:T], head_sq, t - 1, head_sum)

                def head_turn(t):
                    pe.wait_ge(head_normed, t - 1)
                    if t > KVH:
                        pe.wait_ge(head_ready, t - KVH)
                    pe.matmul(ps_rot, turn[:], mix[:, t * T:t * T + TS], start=True, stop=True).then_inc(head_turned, 1)

                q0 = LAYER_Q[layer]
                for t in range(4 * Q_QKV + 2):
                    if t < 4 * Q_QKV:
                        products(q0 + t // 4, t % 4, lambda k: h_hi[:, k, :], lambda k: h_lo[:, k, :], KD,
                                 ready=(h_ready, H_BASE[2 * layer]) if t == 0 else None)
                    if KVH <= t - 1 < 4 * Q_QKV:
                        head_sums(t - 1)
                    if t - 2 >= KVH:
                        head_turn(t - 2)
                for v in range(KVH):
                    turn_v(v)
                pe.wait_ge(v_kept, KVH)
                pe.wait_ge(cache_in, 16)

                def scores(kv, base, n):
                    qt, row = n % 5, tmp[:, 2 + n // 5, :]
                    out = ps_flat[n % 2]
                    if qt == 0:
                        pe.wait_ge(q_held, 2 * base + (n // 5 + 1))
                    if n >= 2:
                        pe.wait_ge(exp_done, 10 * base + (n - 1))
                    key = mix[:, (2 + kv) * T:(3 + kv) * T]
                    if qt < 4:
                        pe.matmul(out[:, 0:TS], row[:, qt * P:(qt + 1) * P], key[:, 0:TS], start=True, stop=True)
                        pe.matmul(out[:, TS:T], row[:, qt * P:(qt + 1) * P], cache_k[:, kv, :], start=True, stop=True).then_inc(score_done, 1)
                    else:
                        pe.matmul(out[:, 0:TP], row[:, TS:T], key[:, TS:T], start=True, stop=True).then_inc(score_done, 1)

                def turn_probs(base, n):
                    pe.wait_ge(prob_ready, 10 * base + (n + 1))
                    if n >= 1:
                        pe.wait_ge(prob_kept, 10 * base + n)
                    for k in range(5 if n % 5 < 4 else 1):
                        mm = pe.transpose(sum_flat[:, k * P:(k + 1) * P], tmp[:, n % 2, k * P:(k + 1) * P], ident[:])
                    mm.then_inc(prob_turned, 1)

                def mix_values(kv, base, hh):
                    pe.wait_ge(prob_kept, 10 * base + (5 * hh + 5))
                    pe.wait_ge(g_ready, 2 * base + (LAYER_G[layer] + hh))
                    for k in range(5):
                        val = v_tok[:, kv, k * P:(k + 1) * P] if k < 4 else cache_v[:, kv, :]
                        pe.matmul(ps_rot, val, prob_s[:, k, :], start=(k == 0), stop=(k == 4))
                    pe.matmul(ps_mixed, v_tok[:, kv, TS:T], prob_p, start=True, stop=True).then_inc(mixed_done, 1)

                for kv in range(KVH):
                    with pe.Fori(2 * kv, 2 * kv + 2) as i:
                        scores(kv, i, 0)
                        scores(kv, i, 1)
                        for n in range(10):
                            if n + 2 < 10:
                                scores(kv, i, n + 2)
                            if n == 5:
                                mix_values(kv, i, 0)
                            turn_probs(i, n)
                        mix_values(kv, i, 1)

            pe.wait_ge(consts_in, CONSTS * 16)
            pe.wait_ge(ones_ready, 2)
            for layer in range(DEPTH):
                q, g, kind = LAYER_Q[layer], LAYER_G[layer], KIND[layer]
                sum_features(sq_sum, sq_added, (KD - 1) * (2 * layer + 1), sum_ready)
                if kind == "conv":
                    with pe.Fori(0, Q_ZU + Q_B) as i:
                        h_quad(i + q, 2 * layer)
                    with pe.Fori(0, Q_OUT) as i:
                        g_quad(i + (q + Q_ZU + Q_B), KD, g)
                elif kind == "pool":
                    for m in range(KD):
                        pair = m // 2 * 2
                        products(q + m // 4, m % 4, lambda k: g_hi[:, pair + k, :], lambda k: g_lo[:, pair + k, :], 2,
                                 ready=(g_ready, g + pair))
                else:
                    attention()
                    with pe.Fori(0, Q_OUT) as i:
                        g_quad(i + (q + Q_QKV), KD, g)
                q += Q_MIX[kind]
                g += G_MIX[kind]
                sum_features(sq_sum, sq_added, (KD - 1) * (2 * layer + 2), sum_ready)
                with pe.Fori(0, 2) as c:
                    with pe.Fori(0, Q_IN) as i:
                        h_quad(c * (Q_IN + Q_OUT) + i + q, 2 * layer + 1)
                    with pe.Fori(0, Q_OUT) as i:
                        g_quad(c * (Q_IN + Q_OUT) + i + (q + Q_IN), CHUNK, c * CHUNK + g)
                q += 2 * (Q_IN + Q_OUT)
                with pe.Fori(0, Q_LAST) as i:
                    h_quad(i + q, 2 * layer + 1)
                with pe.Fori(0, Q_OUT) as i:
                    g_quad(i + (q + Q_LAST), LAST, g + 2 * CHUNK)
            sum_features(sq_sum, sq_added, (KD - 1) * (2 * DEPTH + 1), sum_ready)

        @block.scalar
        def _(act):
            def split_hi(q, j, tiles):
                act.wait_ge(raw_in[j], 16 * q + 16)
                act.activation(w_hi[:, j % 2, 0:tiles * P], raw[:, j, 0:tiles * P], ACT.Copy).then_inc(w_hi_ready, 1)

            def step(q, j, tiles):
                act.wait_ge(unit_done, 4 * q + (j + 1))
                if tiles:
                    split_hi(q + (j + 2) // 4, (j + 2) % 4, tiles)

            def evacuated(q, j):
                return 2 * q + (j // 2 + 2)

            def g_hi_of(src, index):
                act.activation(g_hi[:, index, :], src, ACT.Copy).then_inc(g_hi_ready, 1)

            def ffn_in_quad(q, i, tiles=(KD,) * 4):
                for j in range(4):
                    step(q, j, tiles[j])
                    if j % 2 == 0:
                        for src, dst in parts(0, pair_a[:, j // 2, :]):
                            a = act.activation(dst, src, ACT.Silu)
                        a.then_inc(freed[0], 1)
                    else:
                        act.wait_ge(freed[1], evacuated(q, j))
                        g_hi_of(pair_b[:, j // 2, :], bass.ds(2 * i + j // 2, 1) if not isinstance(i, int) else slice(2 * i + j // 2, 2 * i + j // 2 + 1))

            def out_quad(q, m0, n, tiles, squares):
                for j in range(4):
                    step(q, j, tiles[j])
                    if squares:
                        m = m0 + j
                        act.wait_ge(freed[j % 2], evacuated(q, j))
                        square(m, n)

            def square(m, n):
                if m >= 3:
                    act.wait_ge(sq_added, (KD - 1) * n + m - 2)
                act.activation(sq[:, m % 2, :] if m else sq_sum, x[:, m, :], ACT.Square).then_inc(sq_ready, 1)

            def rms_of(n):
                act.wait_ge(sum_ready, n + 1)
                act.activation(rms[:, 0:TA], ps_sum[:, 0, 0:TA], ACT.Sqrt, bias=eps[:], scale=1.0 / D)
                act.activation(rms[:, TA:T], ps_sum[:, 1, 0:T - TA], ACT.Sqrt, bias=eps[:], scale=1.0 / D).then_inc(rms_ready, 1)

            def normed(layer, which, padded=False):
                n = 2 * layer + which
                rms_of(n)
                shift = ADA_T * layer + KD * (SHIFT1, SHIFT2)[which]
                with act.Fori(0, KD // 2) as i:
                    for s in range(2):
                        act.wait_ge(scaled, 2 * i + (KD * n + s + 1))
                        for g, lo, hi in ((0, 0, TS), (1, TS, T)):
                            if padded:
                                at = (PS0, PP0)[g]
                                dst = mix[:, bass.ds(i * (2 * PW) + (s * PW + at), hi - lo)]
                            else:
                                dst = h_hi[:, bass.ds(2 * i + s, 1), lo:hi]
                            src = pair_b[:, s:s + 1, lo:hi] if not padded else pair_b[:, s, lo:hi]
                            a = act.activation(dst, src, ACT.Identity,
                                               bias=mod[:, bass.ds(2 * i + (shift + s), 1), g:g + 1].rearrange("p a b -> p (a b)"))
                        a.then_inc(h_hi_ready, 1)

            def attention(q0):
                for t in range(4 * Q_QKV + 1):
                    if t < 4 * Q_QKV:
                        step(q0 + t // 4, t % 4, KD)
                        for src, dst in parts(t % 2, mix[:, t * T:(t + 1) * T]):
                            a = act.activation(dst, src, ACT.Copy)
                        a.then_inc(freed[t % 2], 1)
                    if KVH <= t - 1:
                        act.wait_ge(head_sum, t - KVH)
                        if t - 1 > KVH:
                            act.wait_ge(head_normed, t - 1 - KVH)
                        act.activation(head_root[:, 0:TA], ps_sum[:, 0, 0:TA], ACT.Sqrt, bias=eps[:], scale=1.0 / P)
                        act.activation(head_root[:, TA:T], ps_sum[:, 1, 0:T - TA], ACT.Sqrt, bias=eps[:], scale=1.0 / P).then_inc(head_rms, 1)
                    if KVH <= t < 4 * Q_QKV:
                        act.wait_ge(freed[t % 2], evacuated(q0 + t // 4, t % 4))
                        act.activation(tmp[:, t % 2, 0:T], mix[:, t * T:(t + 1) * T], ACT.Square).then_inc(head_sq, 1)

                def softmax_exp(i, n):
                    width = T if n % 5 < 4 else TP
                    act.wait_ge(bias_done, 10 * i + (n + 1))
                    act.activation(tmp[:, n % 2, 0:width], ps_flat[n % 2][:, 0:width], ACT.Exp,
                                   bias=stat[:, 1, n % 2:n % 2 + 1], scale=SCALE,
                                   accum_out=stat[:, 2, n % 2:n % 2 + 1]).then_inc(exp_done, 1)

                def keep_probs(i, n):
                    act.wait_ge(prob_turned, 10 * i + (n + 1))
                    if n == 5:
                        act.wait_ge(mixed_done, 2 * i + 1)
                    if n % 5 < 4:
                        dst = prob_s[:, :, (n % 5) * P:(n % 5 + 1) * P]
                        src = sum_flat[:, 0:T].rearrange("p (k q) -> p k q", k=5)
                    else:
                        dst, src = prob_p, sum_flat[:, 0:P]
                    act.activation(dst, src, ACT.Copy).then_inc(prob_kept, 1)

                def mixed_hi(i, hh):
                    act.wait_ge(mixed_done, 2 * i + (hh + 1))
                    act.activation(g_hi[:, bass.ds(2 * i + hh, 1), 0:TS], ps_rot.rearrange("p (a n) -> p a n", a=1), ACT.Copy)
                    act.activation(g_hi[:, bass.ds(2 * i + hh, 1), TS:T], ps_mixed.rearrange("p (a n) -> p a n", a=1), ACT.Copy).then_inc(g_hi_ready, 1)

                with act.Fori(0, HEADS // 2) as i:
                    softmax_exp(i, 0)
                    for n in range(10):
                        if n + 1 < 10:
                            softmax_exp(i, n + 1)
                        if n == 5:
                            mixed_hi(i, 0)
                        keep_probs(i, n)
                    mixed_hi(i, 1)

            act.wait_ge(consts_in, CONSTS * 16)
            act.wait_ge(ones_ready, 2)
            act.activation(cond[:], cond[:], ACT.Silu).then_inc(cond_ready, 1)
            act.wait_ge(x_in, 16)
            for m in range(KD):
                square(m, 0)
            split_hi(0, 0, KD)
            split_hi(0, 1, KD)
            for layer in range(DEPTH):
                q, g, kind = LAYER_Q[layer], LAYER_G[layer], KIND[layer]
                normed(layer, 0, padded=(kind == "pool"))
                if kind == "conv":
                    with act.Fori(0, Q_ZU) as i:
                        for j in range(4):
                            step(i + q, j, KD)
                            if j % 2 == 0:
                                for src, dst in parts(0, pair_a[:, j // 2, :]):
                                    a = act.activation(dst, src, ACT.Copy)
                                a.then_inc(freed[0], 1)
                    q += Q_ZU
                    with act.Fori(0, Q_B) as i:
                        for j in range(4):
                            step(i + q, j, KD)
                            act.wait_ge(freed[j % 2], evacuated(i + q, j))
                            g_hi_of(pair_b[:, j % 2:j % 2 + 1, :], bass.ds(4 * i + j, 1))
                    q += Q_B
                elif kind == "pool":
                    for k in range(KD):
                        act.wait_ge(diff_ready, k + 1)
                        act.activation(g_hi[:, k, :], pair_b[:, k % 2, :], ACT.Copy).then_inc(g_hi_ready, 1)
                else:
                    attention(q)
                    q += Q_QKV
                last_pair = (2 if kind == "pool" else KD,) * 2 + (KD,) * 2
                out_quad(q, 0, 2 * layer + 1, (2,) * 4 if kind == "pool" else (KD,) * 4, True)
                out_quad(q + 1, 4, 2 * layer + 1, last_pair, True)
                q += Q_OUT
                normed(layer, 1)
                with act.Fori(0, 2) as c:
                    with act.Fori(0, Q_IN) as i:
                        ffn_in_quad(c * (Q_IN + Q_OUT) + i + q, i)
                    with act.Fori(0, Q_OUT) as i:
                        out_quad(c * (Q_IN + Q_OUT) + i + (q + Q_IN), 0, 0, (KD,) * 4, False)
                q += 2 * (Q_IN + Q_OUT)
                with act.Fori(0, Q_LAST - 1) as i:
                    ffn_in_quad(i + q, i)
                q += Q_LAST - 1
                ffn_in_quad(q, Q_LAST - 1, (KD, KD, LAST, LAST))
                q += 1
                after = 0 if layer + 1 == DEPTH else 2 if KIND[layer + 1] == "pool" else KD
                out_quad(q, 0, 2 * layer + 2, (LAST,) * 4, True)
                out_quad(q + 1, 4, 2 * layer + 2, (LAST, LAST, after, after), True)
            rms_of(2 * DEPTH)

        @block.vector
        def _(dve):
            def split_lo(q, j, tiles):
                dve.wait_ge(w_hi_ready, 4 * q + (j + 1))
                dve.tensor_tensor(w_lo[:, j % 2, 0:tiles * P], raw[:, j, 0:tiles * P],
                                  w_hi[:, j % 2, 0:tiles * P].bitcast(F32), ALU.subtract).then_inc(w_lo_ready, 1)

            def step(q, j, tiles):
                if tiles:
                    split_lo(q + (j + 2) // 4, (j + 2) % 4, tiles)
                dve.wait_ge(unit_done, 4 * q + (j + 1))

            def evacuated(q, j):
                return 2 * q + (j // 2 + 2)

            def g_lo_of(src, index, count):
                dve.wait_ge(g_hi_ready, count)
                dve.tensor_tensor(g_lo[:, index, :], src, g_hi[:, index, :].bitcast(F32), ALU.subtract).then_inc(g_ready, 1)
                dve.wait_ge(g_ready, count)

            def ada_tile(qa, j, first=False):
                if j == 0 and not first:
                    dve.wait_ge(ada_kept, qa)
                dve.wait_ge(ada_in[j], 16 * qa + 16)
                for v in range(2):
                    if not first or j or v:
                        dve.wait_ge(ada_step, 2 * ADA_N * qa + (2 * j + v))
                    dve.tensor_tensor_reduce(ada_products, ada_w[:, j * D:(j + 1) * D], cond[:, v, :], 1.0, 0.0,
                                             ALU.mult, ALU.add, ada_raw[:, j, v:v + 1]).then_inc(ada_step, 1)

            def keep_ada(qa):
                dve.wait_ge(ada_step, 2 * ADA_N * qa + 2 * ADA_N)
                dve.tensor_tensor(mod[:, bass.ds(ADA_N * qa, ADA_N), :], ada_raw[:],
                                  mod[:, bass.ds(ADA_N * qa, ADA_N), :], ALU.add).then_inc(ada_kept, 1)

            def ada_in_step(qa, j):
                if qa is not None and j < ADA_N:
                    ada_tile(qa, j)
                    if j == ADA_N - 1:
                        keep_ada(qa)

            def ada_triple(qa, first=False):
                for j in range(ADA_N):
                    ada_tile(qa, j, first)
                keep_ada(qa)

            def gain_of(layer, which):
                dve.wait_ge(ada_kept, ADA_HEAD if layer == 0 and which == 0 else ADA_Q * (layer + 1))
                at = ADA_T * layer + KD * (SCALE1, SCALE2)[which]
                o = KD * (2 * layer + which)
                dve.scalar_tensor_tensor(out=gain[:, o:o + KD, :], in0=mod[:, at:at + KD, :], scalar=1.0,
                                         in1=gain[:, o:o + KD, :], op0=ALU.add, op1=ALU.mult).then_inc(gain_ready, 1)

            def ffn_in_quad(q, i, count, ada=None, tiles=(KD,) * 4):
                for j in range(4):
                    step(q, j, tiles[j])
                    if j % 2:
                        pair = j // 2
                        dve.wait_ge(freed[0], evacuated(q, j))
                        for (src, dst), (_, gate) in zip(parts(1, pair_b[:, pair, :]), parts(1, pair_a[:, pair, :])):
                            v = dve.tensor_tensor(dst, src, gate, ALU.mult)
                        v.then_inc(freed[1], 1)
                        index = slice(2 * i + pair, 2 * i + pair + 1) if isinstance(i, int) else bass.ds(2 * i + pair, 1)
                        g_lo_of(pair_b[:, pair:pair + 1, :], index, count + (pair + 1))
                    ada_in_step(ada, j)

            def out_quad(q, m0, n, gate, tiles, squares, ada=None):
                for j in range(4):
                    step(q, j, tiles[j])
                    for g, (src, dst) in enumerate(parts(j % 2, x[:, m0 + j, :]) if isinstance(m0, int) else
                                                   dynamic_parts(j % 2, m0 + j)):
                        v = dve.scalar_tensor_tensor(out=dst, in0=src, scalar=gate(m0 + j, g), in1=dst,
                                                     op0=ALU.mult, op1=ALU.add)
                    v.then_inc(freed[j % 2], 1)
                    if squares and m0 + j >= 2:
                        add_square(m0 + j - 1, n)
                    ada_in_step(ada, j)
                if squares and m0:
                    add_square(KD - 1, n)

            def dynamic_parts(slot, m):
                row = x[:, bass.ds(m, 1), :].rearrange("p a t -> p (a t)")
                return parts(slot, row)

            def add_square(m, n):
                dve.wait_ge(sq_ready, KD * n + m + 1)
                if m >= 2:
                    dve.wait_ge(sq_added, (KD - 1) * n + m - 1)
                dve.tensor_tensor(sq_sum, sq_sum, sq[:, m % 2, :], ALU.add).then_inc(sq_added, 1)

            def gate_of(block_):
                def gate(m, g):
                    at = ADA_T * layer + KD * block_
                    if isinstance(m, int):
                        return mod[:, at + m, g:g + 1]
                    return mod[:, bass.ds(m + at, 1), g:g + 1].rearrange("p a b -> p (a b)")
                return gate

            def inverse_rms(n):
                dve.wait_ge(rms_ready, n + 1)
                dve.reciprocal(rinv, rms).then_inc(rinv_ready, 1)
                dve.wait_ge(rinv_ready, n + 1)

            def normed(layer, which, padded=False):
                n = 2 * layer + which
                shift = ADA_T * layer + KD * (SHIFT1, SHIFT2)[which]
                inverse_rms(n)
                dve.wait_ge(gain_ready, n + 1)
                with dve.Fori(0, KD // 2) as i:
                    for s in range(2):
                        for g, lo, hi in ((0, 0, TS), (1, TS, T)):
                            v = dve.scalar_tensor_tensor(
                                out=pair_b[:, s:s + 1, lo:hi], in0=x[:, bass.ds(2 * i + s, 1), lo:hi],
                                scalar=gain[:, bass.ds(2 * i + (KD * n + s), 1), g:g + 1].rearrange("p a b -> p (a b)"),
                                in1=tmp[:, 3:4, lo:hi], op0=ALU.mult, op1=ALU.mult)
                        v.then_inc(scaled, 1)
                    for s in range(2):
                        dve.wait_ge(h_hi_ready, 2 * i + (KD * n + s + 1))
                        if padded:
                            continue
                        for g, lo, hi in ((0, 0, TS), (1, TS, T)):
                            v = dve.scalar_tensor_tensor(
                                out=h_lo[:, bass.ds(2 * i + s, 1), lo:hi], in0=pair_b[:, s:s + 1, lo:hi],
                                scalar=mod[:, bass.ds(2 * i + (shift + s), 1), g:g + 1].rearrange("p a b -> p (a b)"),
                                in1=h_hi[:, bass.ds(2 * i + s, 1), lo:hi].bitcast(F32), op0=ALU.add, op1=ALU.subtract)
                        v.then_inc(h_ready, 1)
                    if not padded:
                        dve.wait_ge(h_ready, 2 * i + (H_BASE[n] + 2))

            def conv(layer, q, g):
                ada = layer == 0
                jc = layer // 3
                z = tmp[:, 4:6, 0:CW]
                for at in (0, CS + TS, CP - 1, CW - 1):
                    dve.memset(z[:, :, at:at + 1], 0.0)
                dve.memset(marks[:, 3:4], 0.0).then_inc(pads_ready, 1)
                dve.wait_ge(pads_ready, jc + 1 + (1 if layer > 1 else 0))
                if layer:
                    dve.wait_ge(kv_stored, 32)
                with dve.Fori(0, Q_ZU) as i:
                    for j in range(4):
                        step(i + q, j, KD)
                        if j % 2:
                            pair = j // 2
                            dve.wait_ge(freed[0], evacuated(i + q, j))
                            row = z[:, pair, :]
                            for (src, dst), (_, c) in zip(parts(1, row, CS, CP), parts(1, pair_a[:, pair, :])):
                                v = dve.tensor_tensor(dst, src, c, ALU.mult)
                            v.then_inc(freed[1], 1)
                            dve.wait_ge(freed[1], evacuated(i + q, j))
                            out = mix[:, bass.ds(i * (2 * CW) + (pair * CW + 1), CW - 2)]
                            for n, tap in enumerate((1, 0, 2)):
                                w = conv_w[:, bass.ds(2 * i + ((jc * 3 + tap) * KD + pair), 1)]
                                if n == 0:
                                    v = dve.tensor_scalar(out, row[:, 1:CW - 1], w, None, ALU.mult)
                                else:
                                    dve.wait_ge(conv_step, 6 * i + (jc * 3 * KD + 3 * pair + n))
                                    v = dve.scalar_tensor_tensor(out=out, in0=row[:, tap:tap + CW - 2], scalar=w,
                                                                 in1=out, op0=ALU.mult, op1=ALU.add)
                                v.then_inc(conv_step, 1)
                            dve.wait_ge(conv_step, 6 * i + (jc * 3 * KD + 3 * pair + 3))
                        ada_in_step(i + ADA_HEAD if ada else None, j)
                q += Q_ZU
                dve.wait_ge(conv_step, (jc + 1) * 3 * KD)
                with dve.Fori(0, Q_B) as i:
                    for j in range(4):
                        step(i + q, j, KD)
                        row = mix[:, bass.ds(i * (4 * CW) + j * CW, CW)]
                        for (src, dst), (_, c) in zip(parts(j % 2, pair_b[:, j % 2, :]), parts(j % 2, row, CS, CP)):
                            v = dve.tensor_tensor(dst, src, c, ALU.mult)
                        v.then_inc(freed[j % 2], 1)
                        g_lo_of(pair_b[:, j % 2:j % 2 + 1, :], bass.ds(4 * i + j, 1), 4 * i + (g + j + 1))
                        ada_in_step(i + (ADA_HEAD + Q_ZU) if ada else None, j)
                q += Q_B
                for half in range(Q_OUT):
                    out_quad(q + half, 4 * half, 2 * layer + 1, gate_of(GATE1), (KD,) * 4, True,
                             ada=ADA_HEAD + Q_ZU + Q_B + 2 * half if ada else None)
                    if ada:
                        ada_triple(ADA_HEAD + Q_ZU + Q_B + 2 * half + 1)

            def pooling(layer, q, g):
                steps = [0]

                def chained(ins):
                    ins.then_inc(pool_step, 1)
                    steps[0] += 1
                    dve.wait_ge(pool_step, steps[0])

                normed(layer, 0, padded=True)
                chained(dve.tensor_tensor(pool_gate[:], pool_s[:], mod[:, ADA_T * layer + KD * GATE1:ADA_T * layer + KD * (GATE1 + 1), :], ALU.mult))
                for k in range(KD):
                    h = mix[:, k * PW:(k + 1) * PW]
                    src, a, b = h, tmp[:, 0, :], tmp[:, 1, :]
                    group = k // (KD // len(WINDOWS))
                    w = WINDOWS[group]
                    half, lo, hi = 1, 1, PW
                    chained(dve.tensor_tensor(a[:, lo:hi], src[:, lo - 1:hi - 1], src[:, lo:hi], ALU.add))
                    src = a
                    other = b
                    size = 2
                    while size < w:
                        s = size // 2
                        lo, hi = lo + s, hi - s
                        chained(dve.tensor_tensor(other[:, lo:hi], src[:, lo - s:hi - s], src[:, lo + s:hi + s], ALU.add))
                        src, other = other, src
                        size *= 2
                    for n, (at, length) in enumerate(((PS0, TS), (PP0, TP))):
                        for e, o in enumerate((at, at + length - HP)):
                            v = dve.tensor_tensor(src[:, o:o + HP], src[:, o:o + HP],
                                                  edge[:, group, (2 * n + e) * HP:(2 * n + e + 1) * HP], ALU.mult)
                    chained(v)
                    for at, lo_, n_ in ((PS0, 0, TS), (PP0, TS, TP)):
                        v = dve.scalar_tensor_tensor(out=pair_b[:, k % 2, lo_:lo_ + n_], in0=src[:, at:at + n_], scalar=1.0 / w,
                                                     in1=h[:, at:at + n_], op0=ALU.mult, op1=ALU.subtract)
                    v.then_inc(diff_ready, 1)
                    g_lo_of(pair_b[:, k % 2, :], k, g + k + 1)
                pg = lambda m, g_: pool_gate[:, m, g_:g_ + 1]
                out_quad(q, 0, 2 * layer + 1, pg, (2,) * 4, True)
                out_quad(q + 1, 4, 2 * layer + 1, pg, (2, 2, KD, KD), True)

            def attention(layer, q, g):
                steps = [0]

                def chained(ins):
                    ins.then_inc(head_step, 1)
                    steps[0] += 1
                    dve.wait_ge(head_step, steps[0])

                for t in range(4 * Q_QKV + 2):
                    if t < 4 * Q_QKV:
                        step(q + t // 4, t % 4, KD)
                    if t - 2 >= KVH:
                        row = mix[:, (t - 2) * T:(t - 2) * T + TS]
                        dve.wait_ge(head_turned, t - 3)
                        dve.tensor_tensor(tmp[:, 4, 0:TS], ps_rot, rope[:, 1, :], ALU.mult)
                        chained(dve.tensor_tensor(row, row, rope[:, 0, :], ALU.mult))
                        dve.tensor_tensor(row, row, tmp[:, 4, 0:TS], ALU.add).then_inc(head_ready, 1)
                        dve.wait_ge(head_ready, t - 3)
                    if KVH <= t - 1 < 4 * Q_QKV:
                        row = mix[:, (t - 1) * T:t * T]
                        dve.wait_ge(head_rms, t - KVH)
                        chained(dve.reciprocal(head_root, head_root))
                        w = qk_norm[:, 1:2] if t - 1 < 2 * KVH else qk_norm[:, 0:1]
                        dve.scalar_tensor_tensor(out=row, in0=row, scalar=w, in1=head_root,
                                                 op0=ALU.mult, op1=ALU.mult).then_inc(head_normed, 1)

                for v in range(KVH):
                    dve.wait_ge(v_turned, v + 1)
                    dve.tensor_copy(v_tok[:, v, :], sum_flat[:, 0:T]).then_inc(v_kept, 1)

                def row_max(i, n):
                    width = T if n % 5 < 4 else TP
                    dve.wait_ge(score_done, 10 * i + (n + 1))
                    dve.tensor_reduce(stat[:, 0, n % 2:n % 2 + 1], ps_flat[n % 2][:, 0:width], AX.X, ALU.max).then_inc(max_done, 1)
                    dve.wait_ge(max_done, 10 * i + (n + 1))
                    dve.tensor_scalar(stat[:, 1, n % 2:n % 2 + 1], stat[:, 0, n % 2:n % 2 + 1], -SCALE, None, ALU.mult).then_inc(bias_done, 1)

                def normalise(i, n):
                    width = T if n % 5 < 4 else TP
                    dve.wait_ge(exp_done, 10 * i + (n + 1))
                    dve.reciprocal(stat[:, 3, n % 2:n % 2 + 1], stat[:, 2, n % 2:n % 2 + 1]).then_inc(inv_done, 1)
                    dve.wait_ge(inv_done, 10 * i + (n + 1))
                    dve.tensor_scalar(tmp[:, n % 2, 0:width], tmp[:, n % 2, 0:width], stat[:, 3, n % 2:n % 2 + 1],
                                      None, ALU.mult).then_inc(prob_ready, 1)

                def mixed_lo(i, hh):
                    dve.wait_ge(g_hi_ready, 2 * i + (g + hh + 1))
                    at = bass.ds(2 * i + hh, 1)
                    dve.tensor_tensor(g_lo[:, at, 0:TS], ps_rot.rearrange("p (a n) -> p a n", a=1),
                                      g_hi[:, at, 0:TS].bitcast(F32), ALU.subtract)
                    dve.tensor_tensor(g_lo[:, at, TS:T], ps_mixed.rearrange("p (a n) -> p a n", a=1),
                                      g_hi[:, at, TS:T].bitcast(F32), ALU.subtract).then_inc(g_ready, 1)

                with dve.Fori(0, HEADS // 2) as i:
                    row_max(i, 0)
                    for n in range(10):
                        if n + 1 < 10:
                            row_max(i, n + 1)
                        normalise(i, n)
                        if n == 7:
                            mixed_lo(i, 0)
                    mixed_lo(i, 1)
                q += Q_QKV
                for half in range(Q_OUT):
                    out_quad(q + half, 4 * half, 2 * layer + 1, gate_of(GATE1), (KD,) * 4, True)

            dve.wait_ge(consts_in, CONSTS * 16)
            dve.wait_ge(x_in, 16)
            for m in range(1, KD):
                add_square(m, 0)
            split_lo(0, 0, KD)
            split_lo(0, 1, KD)
            dve.wait_ge(cond_ready, 1)
            ada_triple(0, first=True)
            with dve.Fori(1, ADA_HEAD) as i:
                ada_triple(i)
            gain_of(0, 0)
            for layer in range(DEPTH):
                q, g, kind = LAYER_Q[layer], LAYER_G[layer], KIND[layer]
                if kind == "pool":
                    for o in range(KD):
                        for a, b in ((0, PS0), (PS0 + TS, PP0), (PP0 + TP, PW)):
                            dve.memset(mix[:, o * PW + a:o * PW + b], 0.0)
                    dve.memset(marks[:, 3:4], 0.0).then_inc(pads_ready, 1)
                    dve.wait_ge(pads_ready, 2)
                    pooling(layer, q, g)
                else:
                    normed(layer, 0)
                    (conv if kind == "conv" else attention)(layer, q, g)
                if layer == 0:
                    gain_of(0, 1)
                q += Q_MIX[kind]
                g += G_MIX[kind]
                normed(layer, 1)
                ada = layer + 1 < DEPTH
                qa = ADA_Q * (layer + 1)
                with dve.Fori(0, 2) as c:
                    with dve.Fori(0, Q_IN) as i:
                        ffn_in_quad(c * (Q_IN + Q_OUT) + i + q, i, c * CHUNK + 2 * i + g,
                                    ada=c * (Q_IN + Q_OUT) + i + qa if ada else None)
                    with dve.Fori(0, Q_OUT) as i:
                        out_quad(c * (Q_IN + Q_OUT) + i + (q + Q_IN), 4 * i, 0, gate_of(GATE2), (KD,) * 4, False,
                                 ada=c * (Q_IN + Q_OUT) + i + (qa + Q_IN) if ada else None)
                q += 2 * (Q_IN + Q_OUT)
                qa += 2 * (Q_IN + Q_OUT)
                g += 2 * CHUNK
                with dve.Fori(0, Q_LAST - 1) as i:
                    ffn_in_quad(i + q, i, 2 * i + g, ada=i + qa if ada else None)
                q += Q_LAST - 1
                ffn_in_quad(q, Q_LAST - 1, g + 2 * (Q_LAST - 1), ada=qa + Q_LAST - 1 if ada else None, tiles=(KD, KD, LAST, LAST))
                q += 1
                after = 0 if layer + 1 == DEPTH else 2 if KIND[layer + 1] == "pool" else KD
                out_quad(q, 0, 2 * layer + 2, gate_of(GATE2), (LAST,) * 4, True, ada=qa + Q_LAST if ada else None)
                if ada:
                    gain_of(layer + 1, 0)
                    gain_of(layer + 1, 1)
                out_quad(q + 1, 4, 2 * layer + 2, gate_of(GATE2), (LAST, LAST, after, after), True)
            inverse_rms(2 * DEPTH)
            for k in range(KD):
                dve.scalar_tensor_tensor(out=mix[:, k * T:(k + 1) * T], in0=x[:, k, :], scalar=final_w[:, k:k + 1],
                                         in1=rinv, op0=ALU.mult, op1=ALU.mult).then_inc(y_ready, 1)


def _units(w, order):
    k, n = w.shape
    u = w.reshape(k // P, P, n // P, P).transpose(2, 1, 0, 3)[order].reshape(len(order), P, k)
    if k < KD * P:
        u = np.concatenate([u, np.zeros((len(order), P, KD * P - k), w.dtype)], axis=2)
    return u


def _rows(v):
    return np.moveaxis(v.reshape(*v.shape[:-1], -1, P), -1, 0)


def _twice(v):
    return np.repeat(v[..., None], 2, axis=-1)


def _rope():
    axis = P // 2
    inv = 10000.0 ** (-np.arange(0, axis, 2, dtype=np.float32) / np.float32(axis))
    t = np.arange(TS)
    out = np.zeros((P, 2, TS), np.float32)
    for a, pos in enumerate((t // GRID_W, t % GRID_W)):
        ang = (pos[None, :].astype(np.float32) * inv[:, None].astype(np.float32)).astype(np.float32)
        for half in range(2):
            at = a * axis + half * (axis // 2)
            out[at:at + axis // 2, 0] = np.cos(ang)
            out[at:at + axis // 2, 1] = np.sin(ang)
    return out


def _turn():
    m = np.zeros((P, P), np.float32)
    for a in range(0, P, 64):
        for i in range(32):
            m[a + 32 + i, a + i] = -1.0
            m[a + i, a + 32 + i] = 1.0
    return m


def _edge():
    out = np.ones((P, len(WINDOWS), 4 * HP), np.float32)
    for g, w in enumerate(WINDOWS):
        for n, length in enumerate((TS, TP)):
            for e, start in enumerate((0, length - HP)):
                for i in range(HP):
                    t = start + i
                    count = min(t + w // 2, length) - max(t - w // 2, 0)
                    out[:, g, (2 * n + e) * HP + i] = w / count
    return out


def kernel(**inputs):
    import concourse.bacc as _bacc
    from concourse.bass_utils import run_bass_kernel_spmd as _run

    a = {k: np.asarray(v) for k, v in inputs.items()}
    ffn_in = [np.concatenate([_units(a["ffn_in_w"][i], [n for j in range(FT) for n in (j, FT + j)])]) for i in range(DEPTH)]

    def ffn(i):
        w_out = a["ffn_out_w"][i]
        parts_ = []
        for c in range(3):
            lo, hi = CHUNK * c, min(CHUNK * (c + 1), FT)
            parts_.append(ffn_in[i][2 * lo:2 * hi])
            parts_.append(_units(w_out[lo * P:hi * P], list(range(KD))))
        return parts_

    units = []
    for i in range(DEPTH):
        j = i // 3
        if KIND[i] == "conv":
            units.append(_units(a["conv_in_w"][j], [n for m in range(KD) for n in (KD + m, 2 * KD + m)] + list(range(KD))))
            units.append(_units(a["conv_out_w"][j], list(range(KD))))
        elif KIND[i] == "pool":
            units += [_units(a["pool_w"][j, g], [0, 1]) for g in range(len(WINDOWS))]
        else:
            units.append(_units(a["attn_qkv_w"][j], [10, 11, 8, 9, *range(HEADS)]))
            units.append(_units(a["attn_out_w"][j], list(range(KD))))
        units += ffn(i)
    tokens = np.concatenate([a["x_sample"][0], a["x_prompt"][0]], axis=0)
    arrays = {
        "weights": np.concatenate(units),
        "ada_w": a["ada_w"].transpose(0, 2, 1).reshape(DEPTH * ADA_T, P, D),
        "x": _rows(tokens).transpose(0, 2, 1),
        "cond": np.repeat(np.stack([a["c"][0], a["c_ctx"]])[None], P, axis=0),
        "ada_b": _twice(_rows(a["ada_b"]).reshape(P, -1)),
        "norm_w": _twice(_rows(np.stack([a["norm1_w"], a["norm2_w"]], axis=1)).reshape(P, -1)),
        "ident": np.eye(P, dtype=np.float32),
        "turn": _turn(),
        "conv_w": _rows(a["conv_w"]).reshape(P, -1),
        "qk_norm": np.stack([a["q_norm_w"][0], a["k_norm_w"][0]], axis=-1),
        "final_w": _rows(a["final_norm_w"]),
        "edge": _edge(),
        "pool_s": _twice(_rows(a["pool_scale"][0])),
        "rope": _rope(),
        "cache_k": a["cache_k"][0, 0].transpose(2, 0, 1),
        "cache_v": a["cache_v"][0, 0].transpose(1, 0, 2),
    }
    outs = {"y": (P, KD, T), "new_k": (P, KVH, TP), "new_v": (P, KVH, TP)}
    nc = _bacc.Bacc("TRN2", target_bir_lowering=False, num_devices=1)
    d, feed = {}, {}
    for name, v in arrays.items():
        v = np.ascontiguousarray(v)
        feed["in_" + name] = v
        d[name] = nc.dram_tensor("in_" + name, v.shape, mybir.dt.from_np(v.dtype), kind="ExternalInput").ap()
    for name, shape in outs.items():
        d[name] = nc.dram_tensor("out_" + name, shape, F32, kind="ExternalOutput").ap()
    build(nc, d)
    r = _run(nc, [feed], core_ids=[0]).results[0]
    y = r["out_y"].transpose(2, 1, 0).reshape(T, D)
    new_k = r["out_new_k"].transpose(1, 2, 0)[None, None]
    new_v = r["out_new_v"].transpose(1, 2, 0)[None, None]
    return (np.ascontiguousarray(y[TS:][None]), np.ascontiguousarray(y[:TS][None]),
            np.ascontiguousarray(new_k), np.ascontiguousarray(new_v))
```

```python
from contextlib import ExitStack

import concourse.bass as bass
import numpy as np
from concourse import mybir

F32 = mybir.dt.float32
F32R = mybir.dt.float32r
ALU = mybir.AluOpType
ACT = mybir.ActivationFunctionType
AX = mybir.AxisListType

P = 128
D = 1024
KD = D // P
DEPTH = 4
TS = 512
TP = 128
T = TS + TP
DFF = 2816
FT = DFF // P
CHUNK = 8
LAST = FT - 2 * CHUNK
HEADS = 8
KVH = 2
GRID_W = 64
EPS = 1e-6
SCALE = float(P) ** -0.5
WINDOWS = (2, 4, 8, 16)
NMOD = 6
TA = 256
Q_ZU, Q_B, Q_OUT, Q_QKV, Q_IN, Q_LAST = 4, 2, 2, 3, 4, LAST // 2
Q_FFN = 2 * (Q_IN + Q_OUT) + Q_LAST + Q_OUT
KIND = [("conv", "pool", "attn")[i % 3] for i in range(DEPTH)]
Q_MIX = {"conv": Q_ZU + Q_B + Q_OUT, "pool": Q_OUT, "attn": Q_QKV + Q_OUT}
LAYER_Q = [sum(Q_MIX[KIND[n]] + Q_FFN for n in range(i)) for i in range(DEPTH + 1)]
QUADS = LAYER_Q[DEPTH]
ADA_T = NMOD * KD
ADA_N = 3
ADA_Q = ADA_T // ADA_N
ADA_PE = 3 * ADA_N
ADA_HEAD = -(-(2 * KD - ADA_PE) // ADA_N)
HEAD_SLOTS = 12 * T // D
X_PIECES = 4
G_MIX = {"conv": KD, "pool": 0, "attn": HEADS}
LAYER_G = [sum(G_MIX[KIND[n]] + FT for n in range(i)) for i in range(DEPTH + 1)]
SHIFT1, SCALE1, GATE1, SHIFT2, SCALE2, GATE2 = range(6)
LAYER_P = [sum((KD if KIND[n] == "conv" else 0) + FT for n in range(i)) for i in range(DEPTH + 1)]
LAYER_R = [sum((2 * KD if KIND[n] == "conv" else 0) + FT for n in range(i)) for i in range(DEPTH + 1)]
TH = T + 2
H_BASE = [KD * n for n in range(2 * DEPTH)]
SUMMED = [0] + [2 * i + 1 for i in range(DEPTH) if KIND[i] == "pool"]
CONSTS = 9
CS, CP, CW = 1, TS + 3, T + 4
HP = 8
PS0, PP0, PW = HP, TS + 3 * HP, T + 4 * HP


def build(nc, d):
    with ExitStack() as ctx:
        def sb(name, shape, dt=F32):
            return ctx.enter_context(nc.sbuf_tensor(name, shape, dt))

        def sem(name):
            return ctx.enter_context(nc.semaphore(name))

        x = sb("x", [P, KD, T])
        h_hi = sb("h_hi", [P, KD, TH], F32R)
        h_lo = sb("h_lo", [P, KD, TH], F32R)
        g_hi = sb("g_hi", [P, CHUNK, T], F32R)
        g_lo = sb("g_lo", [P, CHUNK, T], F32R)
        raw = sb("raw", [P, 4, KD * P])
        w_hi = sb("w_hi", [P, 2, KD * P], F32R)
        w_lo = sb("w_lo", [P, 2, KD * P], F32R)
        ada_w = sb("ada_w", [P, ADA_N * D])
        mix = sb("mix", [P, 12 * T])
        tmp = sb("tmp", [P, 6, PW])
        rope = sb("rope", [P, 2, TS])
        cache_v = sb("cache_v", [P, KVH, P])
        ones = sb("ones", [P, P])
        ident = sb("ident", [P, P])
        turn = sb("turn", [P, P])
        mod = sb("mod", [P, DEPTH * ADA_T, 2])
        gain = sb("gain", [P, DEPTH * 2 * KD, 2])
        pool_gate = sb("pool_gate", [P, KD, 2])
        pool_s = sb("pool_s", [P, KD, 2])
        cond = sb("cond", [P, 2, D])
        cond_k = sb("cond_k", [P, KD, 2])
        ada_raw = sb("ada_raw", [P, ADA_N, 2])
        conv_w = sb("conv_w", [P, 2 * 3 * KD])
        qk_norm = sb("qk_norm", [P, 2])
        final_w = sb("final_w", [P, KD])
        edge = sb("edge", [P, len(WINDOWS), 4 * HP])
        eps = sb("eps", [P, 1])
        stat = sb("stat", [P, 4, 2])
        marks = sb("marks", [P, 4])
        bias = sb("bias", [P, 4, 2])
        q_scale = sb("q_scale", [P, HEADS * T // P])

        ps = ctx.enter_context(nc.psum_tensor("ps", [P, 4, 512], F32))
        ps_x = ctx.enter_context(nc.psum_tensor("ps_x", [P, 2, 512], F32))
        ps_sum = ctx.enter_context(nc.psum_tensor("ps_sum", [P, 2, 512], F32))
        ps_rot, ps_mixed = ps_x[:, 0, :], ps_x[:, 1, 0:TP]
        turned = ps_x[:, 1, 0:TS]
        ada_products = ps_x[:].rearrange("p b n -> p (b n)")
        sum_flat = ps_sum[:].rearrange("p b n -> p (b n)")
        ps_flat = [ps[:, 2 * s:2 * s + 2, :].rearrange("p b n -> p (b n)") for s in range(2)]
        prob_t = ada_w[:]
        prob_s = prob_t[:, 0:5 * TS].rearrange("p (k q) -> p k q", k=5)
        prob_p = prob_t[:, 5 * TS:5 * TS + TP]
        prob_odd = raw[:, 1:4, :].rearrange("p k t -> p (k t)")
        prob_of = [(prob_s, prob_p), (prob_odd[:, 0:5 * TS].rearrange("p (k q) -> p k q", k=5), prob_odd[:, 5 * TS:5 * TS + TP])]
        cache_k = prob_t[:, 5 * TS + TP:5 * TS + TP + KVH * P].rearrange("p (h k) -> p h k", h=KVH)
        v_tok = tmp[:, 4:6, 0:T]
        sq, sq_sum, rms, rinv = tmp[:, 0:2, 0:T], tmp[:, 2, 0:T], tmp[:, 3, 0:T], tmp[:, 3, 0:T]
        head_root = tmp[:, 5, 0:T]
        pair_a, pair_b = tmp[:, 0:2, 0:T], tmp[:, 4:6, 0:T]

        head_w = mix[:, 0:HEAD_SLOTS * D].rearrange("p (n c) -> p n c", n=HEAD_SLOTS)
        head_out = ps[:, 3, 0:2 * ADA_PE].rearrange("p (n v) -> p n v", v=2)
        pool_rows = mix[:, 0:4 * PW].rearrange("p (r c) -> p r c", r=4)
        window_a = mix[:, 4 * PW:6 * PW].rearrange("p (r c) -> p r c", r=2)
        window_b = mix[:, 6 * PW:8 * PW].rearrange("p (r c) -> p r c", r=2)

        cond_in = sem("cond_in")
        consts_in = sem("consts_in")
        late_in = sem("late_in")
        head_in = [sem(f"head_in{j}") for j in range(HEAD_SLOTS)]
        head_tile = sem("head_tile")
        head_kept = sem("head_kept")
        pool_gate_ready = sem("pool_gate_ready")
        pooled_ready = sem("pooled_ready")
        cache_in = sem("cache_in")
        x_in = sem("x_in")
        raw_in = [sem(f"raw_in{j}") for j in range(4)]
        ada_in = [sem(f"ada_in{j}") for j in range(ADA_N)]
        w_hi_ready = sem("w_hi_ready")
        w_lo_ready = sem("w_lo_ready")
        unit_done = sem("unit_done")
        freed = [sem("even_freed"), sem("odd_freed")]
        ada_step = sem("ada_step")
        ada_kept = sem("ada_kept")
        cond_ready = sem("cond_ready")
        gain_ready = sem("gain_ready")
        ones_ready = sem("ones_ready")
        sq_ready = sem("sq_ready")
        sq_added = sem("sq_added")
        sum_ready = sem("sum_ready")
        rms_ready = sem("rms_ready")
        rinv_ready = sem("rinv_ready")
        shift_hi_ready = sem("shift_hi_ready")
        shift_ready = sem("shift_ready")
        gate_ready = sem("gate_ready")
        product_ready = sem("product_ready")
        row_ready = sem("row_ready")
        h_hi_ready = sem("h_hi_ready")
        h_ready = sem("h_ready")
        g_hi_ready = sem("g_hi_ready")
        g_ready = sem("g_ready")
        pads_ready = sem("pads_ready")
        conv_step = sem("conv_step")
        pool_step = sem("pool_step")
        head_step = sem("head_step")
        v_turned = sem("v_turned")
        v_kept = sem("v_kept")
        head_sq = sem("head_sq")
        head_sum = sem("head_sum")
        head_rms = sem("head_rms")
        head_normed = sem("head_normed")
        head_turned = sem("head_turned")
        head_ready = sem("head_ready")
        q_held = sem("q_held")
        score_done = sem("score_done")
        max_done = sem("max_done")
        bias_done = sem("bias_done")
        exp_done = sem("exp_done")
        inv_done = sem("inv_done")
        prob_ready = sem("prob_ready")
        prob_turned = sem("prob_turned")
        prob_kept = sem("prob_kept")
        mixed_done = sem("mixed_done")
        kv_stored = sem("kv_stored")
        y_ready = sem("y_ready")
        y_stored = sem("y_stored")

        block = ctx.enter_context(nc.Block())

        def sample_of(slot):
            return ps[:, 2 * slot:2 * slot + 2, 0:TA]

        def prompt_of(slot):
            return ps[:, 2 * slot + 1, TA:TA + TP]

        def at_(index):
            return slice(index, index + 1) if isinstance(index, int) else bass.ds(index, 1)

        def halves(row):
            return row.rearrange("p (b n) -> p b n", b=2)

        def parts(slot, row, off_s=0, off_p=TS):
            return ((sample_of(slot), halves(row[:, off_s:off_s + TS])),
                    (prompt_of(slot), row[:, off_p:off_p + TP]))

        def groups(row):
            return row[:, 0:TS], row[:, TS:T]

        @block.sync
        def _(sp):
            def load_consts():
                for dst, name in ((mod, "ada_b"), (gain, "norm_w"), (ident, "ident"),
                                  (turn, "turn"), (conv_w, "conv_w"), (qk_norm, "qk_norm"),
                                  (final_w, "final_w"), (edge, "edge"), (pool_s, "pool_s")):
                    sp.dma_start(dst[:], d[name]).then_inc(consts_in, 16)

            def load_head(n):
                if n >= HEAD_SLOTS:
                    sp.wait_ge(head_tile, n - HEAD_SLOTS + 1)
                sp.dma_start(head_w[:, n % HEAD_SLOTS, :], d["ada_head"][n]).then_inc(head_in[n % HEAD_SLOTS], 16)

            def load_raw(q, units):
                for j in units:
                    sp.dma_start(raw[:, j, :], d["weights"][4 * q + j]).then_inc(raw_in[j], 16)

            def load(q, tiles, units=range(4)):
                for j in units:
                    sp.wait_ge(w_lo_ready, 4 * q + (j - 3))
                    sp.dma_start(raw[:, j, 0:tiles * P], d["weights"][4 * q + j, :, 0:tiles * P]).then_inc(raw_in[j], 16)

            sp.dma_start(cond[:], d["cond"]).then_inc(cond_in, 16)
            sp.dma_start(cond_k[:], d["cond_k"]).then_inc(cond_in, 16)
            for n in range(ADA_PE):
                if n > 1:
                    sp.wait_ge(ada_step, 2 * n - 2)
                load_head(n)
                if n == 1:
                    load_consts()
                if 0 < n <= X_PIECES:
                    piece = slice((n - 1) * KD // X_PIECES, n * KD // X_PIECES)
                    sp.dma_start(x[:, piece, :], d["x"][:, piece, :]).then_inc(x_in, 16)
                if n == ADA_PE - 3:
                    load_raw(0, (0, 1))
            load_raw(0, (2, 3))
            for dst, name in ((rope, "rope"), (cache_v, "cache_v")):
                sp.dma_start(dst[:], d[name]).then_inc(late_in, 16)
            for layer in range(DEPTH):
                q = LAYER_Q[layer]
                kind = KIND[layer]
                if layer == 0:
                    with sp.Fori(1, Q_MIX[kind]) as i:
                        load(i, KD)
                elif kind == "pool":
                    load(q, 2)
                    load(q + 1, 2)
                else:
                    if kind == "attn":
                        sp.wait_ge(ada_step, 2 * (ADA_N * ADA_Q * (layer + 1) - ADA_PE))
                        sp.dma_start(cache_k, d["cache_k"]).then_inc(cache_in, 16)
                    with sp.Fori(0, Q_QKV if kind == "attn" else Q_MIX[kind]) as i:
                        load(i + q, KD)
                if kind == "attn":
                    load(q + Q_QKV, KD, (0, 1))
                    sp.wait_ge(head_ready, KVH)
                    sp.dma_start(d["new_v"], mix[:, 0:2 * T].rearrange("p (h t) -> p h t", h=KVH)[:, :, TS:T]).then_inc(kv_stored, 16)
                    sp.dma_start(d["new_k"], mix[:, 2 * T:4 * T].rearrange("p (h t) -> p h t", h=KVH)[:, :, TS:T]).then_inc(kv_stored, 16)
                    sp.wait_ge(mixed_done, HEADS)
                    load(q + Q_QKV, KD, (2, 3))
                    load(q + Q_QKV + 1, KD)
                q += Q_MIX[kind]
                with sp.Fori(0, 2 * (Q_IN + Q_OUT)) as i:
                    load(i + q, KD)
                q += 2 * (Q_IN + Q_OUT)
                with sp.Fori(0, Q_LAST) as i:
                    load(i + q, KD)
                q += Q_LAST
                with sp.Fori(0, Q_OUT) as i:
                    load(i + q, LAST)
            for k in range(KD):
                sp.wait_ge(y_ready, k + 1)
                sp.dma_start(d["y"][:, k, :], mix[:, k * T:(k + 1) * T]).then_inc(y_stored, 16)
            sp.wait_ge(kv_stored, 32)
            sp.wait_ge(y_stored, 16 * KD)

        @block.gpsimd
        def _(pool):
            pool.memset(ones[:], 1.0).then_inc(ones_ready, 1)
            pool.memset(eps[:], EPS).then_inc(ones_ready, 1)
            for n, free in enumerate(freed):
                pool.memset(marks[:, n:n + 1], 0.0).then_inc(free, 1)

            def load_ada(qa, j, first=False):
                if not first:
                    pool.wait_ge(ada_step, 2 * ADA_N * qa + (2 * j + 2 - 2 * ADA_N))
                pool.dma_start(ada_w[:, j * D:(j + 1) * D], d["ada_w"][ADA_N * qa + j]).then_inc(ada_in[j], 16)

            def hold(h, s):
                pool.wait_ge(head_ready, h + (KVH + 1))
                pool.tensor_copy(tmp[:, 2 + s, 0:T], mix[:, bass.ds(h * T + 4 * T, T)]).then_inc(q_held, 1)

            for j in range(ADA_N):
                load_ada(0, j, first=True)
            attn_q = ADA_Q * (KIND.index("attn") + 1) - ADA_PE // ADA_N
            with pool.Fori(1, attn_q) as i:
                for j in range(ADA_N):
                    load_ada(i, j)
            hold(0, 0)
            pool.wait_ge(head_ready, HEADS + KVH)
            hold(1, 1)
            with pool.Fori(1, HEADS // 2) as i:
                for s in range(2):
                    pool.wait_ge(score_done, 10 * i + (5 * s - 5))
                    hold(2 * i + s, s)
            pool.wait_ge(mixed_done, HEADS)
            with pool.Fori(attn_q, ADA_Q * DEPTH - ADA_PE // ADA_N) as i:
                for j in range(ADA_N):
                    load_ada(i, j)

        @block.tensor
        def _(pe):
            def products(q, j, a_hi, a_lo, tiles, width=T, ready=None, norm=None):
                slot = j % 2
                pe.wait_ge(w_lo_ready, 4 * q + (j + 1))
                pe.wait_ge(freed[slot], 2 * q + (j // 2 + 1))
                for k in range(tiles):
                    if k >= tiles - 2 and norm in SUMMED:
                        if norm:
                            for m in (2 * k - tiles, 2 * k - tiles + 1):
                                sum_squares(norm, m)
                    elif k == tiles - 1 and norm is not None:
                        sum_features(sq_sum, sq_added, (KD - 1) * (norm + 1), sum_ready)
                    if ready is not None:
                        pe.wait_ge(ready[0], ready[1] + k + 1)
                    ws = slice(k * P, k * P + P)
                    passes = ((w_hi, a_hi), (w_hi, a_lo), (w_lo, a_hi))
                    for n, (w, a) in enumerate(passes):
                        begin, end = k == 0 and n == 0, k == tiles - 1 and n == 2
                        pe.matmul(ps[:, 2 * slot, 0:TA], w[:, slot, ws], a(k)[:, 0:TA], start=begin, stop=end)
                        mm = pe.matmul(ps[:, 2 * slot + 1, 0:width - TA], w[:, slot, ws], a(k)[:, TA:width], start=begin, stop=end)
                mm.then_inc(unit_done, 1)

            def h_unit(q, j, n, first=False):
                if j == 0 and first:
                    pe.wait_ge(shift_ready, H_BASE[n] // KD + 1)
                products(q, j, lambda k: h_hi[:, k, :], lambda k: h_lo[:, k, :], KD, width=TH,
                         ready=(h_ready, H_BASE[n]) if j == 0 else None, norm=n if j == 0 and first else None)

            def h_quads(q, n, count, first=True):
                if first:
                    for j in range(4):
                        h_unit(q, j, n, first=True)
                with pe.Fori(1 if first else 0, count) as i:
                    for j in range(4):
                        h_unit(i + q, j, n)

            def g_quad(q, tiles, base):
                for j in range(4):
                    products(q, j, lambda k: g_hi[:, k, :], lambda k: g_lo[:, k, :], tiles,
                             ready=(g_ready, base) if j == 0 else None)

            def sum_features(src, s, value, done):
                pe.wait_ge(s, value)
                pe.matmul(ps_sum[:, 0, 0:TA], ones[:], src[:, 0:TA], start=True, stop=True)
                pe.matmul(ps_sum[:, 1, 0:T - TA], ones[:], src[:, TA:T], start=True, stop=True).then_inc(done, 1)

            def sum_squares(n, m):
                pe.wait_ge(sq_ready, KD * n + m + 1)
                src = sq[:, m % 2, :] if m else sq_sum
                begin, end = m == 0, m == KD - 1
                mm = pe.matmul(ps_sum[:, 0, 0:TA], ones[:], src[:, 0:TA], start=begin, stop=end)
                if end:
                    mm.then_inc(sq_added, 1)
                mm = pe.matmul(ps_sum[:, 1, 0:T - TA], ones[:], src[:, TA:T], start=begin, stop=end)
                if m:
                    mm.then_inc(sum_ready if end else sq_added, 1)

            def attention():
                def turn_v(v):
                    pe.wait_ge(head_rms, HEADS + KVH)
                    if v:
                        pe.wait_ge(v_kept, v)
                    for k in range(T // P):
                        mm = pe.transpose(sum_flat[:, k * P:(k + 1) * P], mix[:, v * T + k * P:v * T + (k + 1) * P], ident[:])
                    mm.then_inc(v_turned, 1)

                def head_sums(t):
                    pe.wait_ge(head_sq, t - 1)
                    if t > KVH:
                        pe.wait_ge(head_rms, t - KVH)
                    row = tmp[:, t % 2, 0:T]
                    if t < 2 * KVH:
                        pe.matmul(ps_sum[:, 0, 0:TA], ones[:], row[:, 0:TA], start=True, stop=True)
                        mm = pe.matmul(ps_sum[:, 1, 0:T - TA], ones[:], row[:, TA:T], start=True, stop=True)
                    else:
                        for k in range(T // P):
                            mm = pe.matmul(ps_sum[:, 0, k:k + 1], row[:, k * P:(k + 1) * P], ones[:, 0:1], start=True, stop=True)
                    mm.then_inc(head_sum, 1)

                def head_turn(t):
                    pe.wait_ge(head_normed, t - 1)
                    if t > KVH:
                        pe.wait_ge(head_ready, t - KVH)
                    pe.matmul(ps_rot, turn[:], mix[:, t * T:t * T + TS], start=True, stop=True).then_inc(head_turned, 1)

                def scores(kv, base, n):
                    qt, row = n % 5, tmp[:, 2 + n // 5, :]
                    out = ps_flat[n % 2]
                    if qt == 0:
                        pe.wait_ge(q_held, 2 * base + (n // 5 + 1))
                    if base or n >= 2:
                        pe.wait_ge(exp_done, 10 * base + (n - 1))
                    key = mix[:, (2 + kv) * T:(3 + kv) * T]
                    if qt < 4:
                        pe.matmul(out[:, 0:TS], row[:, qt * P:(qt + 1) * P], key[:, 0:TS], start=True, stop=True)
                        pe.matmul(out[:, TS:T], row[:, qt * P:(qt + 1) * P], cache_k[:, kv, :], start=True, stop=True).then_inc(score_done, 1)
                    else:
                        pe.matmul(out[:, 0:TP], row[:, TS:T], key[:, TS:T], start=True, stop=True).then_inc(score_done, 1)

                def turn_probs(base, n):
                    pe.wait_ge(prob_ready, 10 * base + (n + 1))
                    if base or n >= 1:
                        pe.wait_ge(prob_kept, 10 * base + n)
                    for k in range(5 if n % 5 < 4 else 1):
                        mm = pe.transpose(sum_flat[:, k * P:(k + 1) * P], tmp[:, n % 2, k * P:(k + 1) * P], ident[:])
                    mm.then_inc(prob_turned, 1)

                def mix_values(kv, base, hh):
                    pe.wait_ge(prob_kept, 10 * base + (5 * hh + 5))
                    pe.wait_ge(g_ready, 2 * base + (LAYER_G[layer] + hh))
                    of_sample, of_prompt = prob_of[hh]
                    for k in range(5):
                        val = v_tok[:, kv, k * P:(k + 1) * P] if k < 4 else cache_v[:, kv, :]
                        pe.matmul(ps_rot, val, of_sample[:, k, :], start=(k == 0), stop=(k == 4))
                    pe.matmul(ps_mixed, v_tok[:, kv, TS:T], of_prompt, start=True, stop=True).then_inc(mixed_done, 1)

                q0 = LAYER_Q[layer]
                for t in range(4 * Q_QKV + 2):
                    if t < 4 * Q_QKV:
                        h_unit(q0 + t // 4, t % 4, 2 * layer, first=(t == 0))
                    if t == 4 * Q_QKV:
                        pe.wait_ge(row_ready, KD + 4 * Q_QKV - 1)
                        pe.wait_ge(cache_in, 16)
                        scores(0, 0, 0)
                    if KVH <= t - 1 < 4 * Q_QKV:
                        head_sums(t - 1)
                    if t - 2 >= KVH:
                        head_turn(t - 2)
                    if t >= 4 * Q_QKV:
                        if t > 4 * Q_QKV:
                            pe.wait_ge(row_ready, KD + 4 * Q_QKV)
                            scores(0, 0, 1)
                        turn_v(t - 4 * Q_QKV)
                pe.wait_ge(v_kept, KVH)
                pe.wait_ge(late_in, 32)

                for pair in range(HEADS // 2):
                    for n in range(10):
                        ahead = 10 * pair + n + 2
                        if ahead < 5 * HEADS:
                            scores(ahead // 10 * KVH // (HEADS // 2), ahead // 10, ahead % 10)
                        if n == 1 and pair:
                            mix_values((pair - 1) * KVH // (HEADS // 2), pair - 1, 1)
                        if n == 6:
                            mix_values(pair * KVH // (HEADS // 2), pair, 0)
                        turn_probs(pair, n)
                mix_values(KVH - 1, HEADS // 2 - 1, 1)

            pe.wait_ge(cond_ready, 2)
            for n in range(ADA_PE):
                pe.wait_ge(head_in[n % HEAD_SLOTS], 16 * (n // HEAD_SLOTS) + 16)
                if n == ADA_PE - KD // 2:
                    pe.wait_ge(ones_ready, 2)
                if n >= ADA_PE - KD // 2:
                    for m in (2 * (n - ADA_PE) + KD, 2 * (n - ADA_PE) + KD + 1):
                        sum_squares(0, m)
                for k in range(KD):
                    mm = pe.matmul(head_out[:, n, :], head_w[:, n % HEAD_SLOTS, k * P:(k + 1) * P], cond_k[:, k, :],
                                   start=(k == 0), stop=(k == KD - 1))
                mm.then_inc(head_tile, 1)
            pe.wait_ge(consts_in, CONSTS * 16)
            for layer in range(DEPTH):
                q, g, kind = LAYER_Q[layer], LAYER_G[layer], KIND[layer]
                if kind == "conv":
                    h_quads(q, 2 * layer, Q_ZU + Q_B)
                    with pe.Fori(0, Q_OUT) as i:
                        g_quad(i + (q + Q_ZU + Q_B), KD, g)
                elif kind == "pool":
                    pe.wait_ge(shift_ready, 2 * layer + 1)
                    for m in range(KD):
                        pair = m // 2 * 2
                        products(q + m // 4, m % 4, lambda k: h_hi[:, pair + k, :], lambda k: h_lo[:, pair + k, :], 2,
                                 width=TH, ready=(h_ready, H_BASE[2 * layer] + pair))
                        if m == 0:
                            sum_features(sq_sum, sq_added, (KD - 1) * (2 * layer + 1), sum_ready)
                        elif m > 3 and m % 2:
                            sum_squares(2 * layer + 1, m - 5)
                            sum_squares(2 * layer + 1, m - 4)
                else:
                    attention()
                    with pe.Fori(0, Q_OUT) as i:
                        g_quad(i + (q + Q_QKV), KD, g)
                q += Q_MIX[kind]
                g += G_MIX[kind]
                for c in range(3):
                    tiles = CHUNK if c < 2 else LAST
                    h_quads(q, 2 * layer + 1, tiles // 2, first=(c == 0))
                    q += tiles // 2
                    with pe.Fori(0, Q_OUT) as i:
                        g_quad(i + q, tiles, g)
                    q += Q_OUT
                    g += tiles
            sum_features(sq_sum, sq_added, (KD - 1) * (2 * DEPTH + 1), sum_ready)

        @block.scalar
        def _(act):
            def split_hi(q, j, tiles):
                act.wait_ge(raw_in[j], 16 * q + 16)
                act.activation(w_hi[:, j % 2, 0:tiles * P], raw[:, j, 0:tiles * P], ACT.Copy).then_inc(w_hi_ready, 1)

            def step(q, j, tiles):
                act.wait_ge(unit_done, 4 * q + (j + 1))
                if tiles:
                    split_hi(q + (j + 2) // 4, (j + 2) % 4, tiles)

            def evacuated(q, j):
                return 2 * q + (j // 2 + 2)

            def g_hi_of(src, index):
                act.activation(g_hi[:, index, :], src, ACT.Copy).then_inc(g_hi_ready, 1)

            def gate(q, j, func):
                act.wait_ge(freed[0], evacuated(q, j))
                for g, row in enumerate(groups(pair_a[:, j // 2, :])):
                    a = act.activation(row, row, func, bias=bias[:, j, g:g + 1])
                a.then_inc(gate_ready, 1)

            def ffn_in_quad(q, i, products, tiles=(KD,) * 4):
                for j in range(4):
                    step(q, j, tiles[j])
                    if j % 2 == 0:
                        gate(q, j, ACT.Silu)
                    else:
                        act.wait_ge(product_ready, products + (j // 2 + 1))
                        g_hi_of(pair_b[:, j // 2, :], bass.ds(2 * i + j // 2, 1) if not isinstance(i, int) else slice(2 * i + j // 2, 2 * i + j // 2 + 1))

            def out_quad(q, m0, n, tiles, squares, folds=True):
                for j in range(4):
                    m = m0 + j
                    late = squares and m == KD - 1
                    if not late:
                        step(q, j, tiles[j])
                    if squares:
                        act.wait_ge(freed[j % 2], evacuated(q, j))
                        square(m, n)
                        if folds:
                            fold_hi(m, n)
                    if late:
                        step(q, j, tiles[j])

            def fold_hi(m, n):
                for g, (row, src) in enumerate(zip(groups(h_hi[:, m, 0:T]), groups(x[:, m, :]))):
                    a = act.activation(row, src, ACT.Identity, scale=gain[:, KD * n + m, g:g + 1])
                a.then_inc(h_hi_ready, 1)

            def shift_hi(n):
                act.wait_ge(gain_ready, n + 1)
                at = ADA_T * (n // 2) + KD * (SHIFT1, SHIFT2)[n % 2]
                act.activation(h_hi[:, :, T:TH], mod[:, at:at + KD, :], ACT.Copy).then_inc(shift_hi_ready, 1)

            def square(m, n):
                if m >= 3:
                    act.wait_ge(sq_added, (KD - 1) * n + m - 2)
                act.activation(sq[:, m % 2, :] if m else sq_sum, x[:, m, :], ACT.Square).then_inc(sq_ready, 1)

            def rms_of(n):
                act.wait_ge(sum_ready, n + 1)
                act.activation(rms[:, 0:TA], ps_sum[:, 0, 0:TA], ACT.Sqrt, bias=eps[:], scale=1.0 / D)
                act.activation(rms[:, TA:T], ps_sum[:, 1, 0:T - TA], ACT.Sqrt, bias=eps[:], scale=1.0 / D).then_inc(rms_ready, 1)

            def pooling(layer, q):
                n = 2 * layer + 1

                def split(group):
                    for m in (2 * group, 2 * group + 1):
                        if m < KD - 1:
                            step(q + m // 4, m % 4, 2 if m < KD - 2 else KD)

                def shifted(group):
                    for m in (2 * group, 2 * group + 1):
                        act.wait_ge(freed[m % 2], evacuated(q + m // 4, m % 4))
                        row = pool_rows[:, m % 4, :]
                        for g, (at, length) in enumerate(((PS0, TS), (PP0, TP))):
                            a = act.activation(row[:, at:at + length], row[:, at:at + length], ACT.Identity, bias=bias[:, m % 4, g:g + 1])
                        a.then_inc(row_ready, 1)

                def fold(group):
                    for m in (2 * group, 2 * group + 1):
                        act.wait_ge(pooled_ready, m + 1)
                        fold_hi(m, n)
                        square(m, n)

                rms_of(2 * layer)
                split(0)
                shifted(0)
                split(1)
                shifted(1)
                split(2)
                fold(0)
                shifted(2)
                split(3)
                act.wait_ge(unit_done, 4 * q + KD)
                shift_hi(n)
                fold(1)
                shifted(3)
                fold(2)
                fold(3)
                split_hi(q + 2, 1, KD)

            def attention(q0):
                for t in range(4 * Q_QKV + 1):
                    if t < 4 * Q_QKV:
                        step(q0 + t // 4, t % 4, KD)
                        act.wait_ge(freed[t % 2], evacuated(q0 + t // 4, t % 4))
                        for g, row in enumerate(groups(mix[:, t * T:(t + 1) * T])):
                            a = act.activation(row, row, ACT.Identity, bias=bias[:, t % 4, g:g + 1])
                        a.then_inc(row_ready, 1)
                    if KVH <= t - 1:
                        act.wait_ge(head_sum, t - KVH)
                        if t - 1 > KVH:
                            act.wait_ge(head_normed, t - 1 - KVH)
                        if t - 1 < 2 * KVH:
                            act.activation(head_root[:, 0:TA], ps_sum[:, 0, 0:TA], ACT.Sqrt, bias=eps[:], scale=1.0 / P)
                            a = act.activation(head_root[:, TA:T], ps_sum[:, 1, 0:T - TA], ACT.Sqrt, bias=eps[:], scale=1.0 / P)
                        else:
                            at = (t - 1 - 2 * KVH) * (T // P)
                            a = act.activation(q_scale[:, at:at + T // P], ps_sum[:, 0, 0:T // P], ACT.Sqrt, bias=eps[:], scale=1.0 / P)
                        a.then_inc(head_rms, 1)
                    if KVH <= t < 4 * Q_QKV:
                        act.wait_ge(row_ready, KD + t + 1)
                        act.activation(tmp[:, t % 2, 0:T], mix[:, t * T:(t + 1) * T], ACT.Square).then_inc(head_sq, 1)

                def softmax_exp(i, n):
                    width = T if n % 5 < 4 else TP
                    act.wait_ge(bias_done, 10 * i + (n + 1))
                    act.activation(tmp[:, n % 2, 0:width], ps_flat[n % 2][:, 0:width], ACT.Exp,
                                   bias=stat[:, 1, n % 2:n % 2 + 1], scale=q_scale[:, at_(i * (2 * T // P) + n)],
                                   accum_out=stat[:, 2, n % 2:n % 2 + 1]).then_inc(exp_done, 1)

                def keep_probs(i, n):
                    act.wait_ge(prob_turned, 10 * i + (n + 1))
                    of_sample, of_prompt = prob_of[n // 5]
                    if n % 5 < 4:
                        dst = of_sample[:, :, (n % 5) * P:(n % 5 + 1) * P]
                        src = sum_flat[:, 0:T].rearrange("p (k q) -> p k q", k=5)
                    else:
                        dst, src = of_prompt, sum_flat[:, 0:P]
                    act.activation(dst, src, ACT.Copy).then_inc(prob_kept, 1)

                def mixed_hi(i, hh):
                    act.wait_ge(mixed_done, 2 * i + (hh + 1))
                    act.activation(g_hi[:, at_(2 * i + hh), 0:TS], ps_rot.rearrange("p (a n) -> p a n", a=1), ACT.Copy)
                    act.activation(g_hi[:, at_(2 * i + hh), TS:T], ps_mixed.rearrange("p (a n) -> p a n", a=1), ACT.Copy).then_inc(g_hi_ready, 1)

                def pair(i, first=False, last=False):
                    for n in range(10):
                        if n + 1 < 10 or not last:
                            softmax_exp(i, n + 1)
                        keep_probs(i, n)
                        if n == 1 and not first:
                            mixed_hi(i - 1, 1)
                        if n == 6:
                            mixed_hi(i, 0)

                softmax_exp(0, 0)
                pair(0, first=True)
                with act.Fori(1, HEADS // 2 - 1) as i:
                    pair(i)
                pair(HEADS // 2 - 1, last=True)
                mixed_hi(HEADS // 2 - 1, 1)

            act.wait_ge(cond_in, 32)
            act.activation(cond[:], cond[:], ACT.Silu).then_inc(cond_ready, 1)
            act.activation(cond_k[:], cond_k[:], ACT.Silu).then_inc(cond_ready, 1)
            act.wait_ge(consts_in, CONSTS * 16)
            act.wait_ge(ones_ready, 2)
            act.wait_ge(x_in, 16 * X_PIECES)
            for m in range(KD):
                square(m, 0)
            split_hi(0, 0, KD)
            split_hi(0, 1, KD)
            shift_hi(0)
            for m in range(KD):
                fold_hi(m, 0)
            for layer in range(DEPTH):
                q, g, kind, r = LAYER_Q[layer], LAYER_G[layer], KIND[layer], LAYER_R[layer]
                if kind != "pool":
                    rms_of(2 * layer)
                if kind == "conv":
                    with act.Fori(0, Q_ZU) as i:
                        for j in range(4):
                            step(i + q, j, KD)
                            if j % 2 == 0:
                                gate(i + q, j, ACT.Identity)
                    q += Q_ZU
                    r += KD
                    with act.Fori(0, Q_B) as i:
                        for j in range(4):
                            step(i + q, j, KD)
                            act.wait_ge(product_ready, 4 * i + (r + j + 1))
                            g_hi_of(pair_b[:, j % 2:j % 2 + 1, :], bass.ds(4 * i + j, 1))
                    q += Q_B
                    r += KD
                elif kind == "pool":
                    pooling(layer, q)
                else:
                    attention(q)
                    q += Q_QKV
                if kind != "pool":
                    shift_hi(2 * layer + 1)
                    out_quad(q, 0, 2 * layer + 1, (KD,) * 4, True)
                    out_quad(q + 1, 4, 2 * layer + 1, (KD,) * 4, True)
                q += Q_OUT
                rms_of(2 * layer + 1)
                with act.Fori(0, 2) as c:
                    with act.Fori(0, Q_IN) as i:
                        ffn_in_quad(c * (Q_IN + Q_OUT) + i + q, i, c * CHUNK + 2 * i + r)
                    with act.Fori(0, Q_OUT) as i:
                        out_quad(c * (Q_IN + Q_OUT) + i + (q + Q_IN), 0, 0, (KD,) * 4, False)
                q += 2 * (Q_IN + Q_OUT)
                r += 2 * CHUNK
                with act.Fori(0, Q_LAST - 1) as i:
                    ffn_in_quad(i + q, i, 2 * i + r)
                q += Q_LAST - 1
                ffn_in_quad(q, Q_LAST - 1, r + 2 * (Q_LAST - 1), (KD, KD, LAST, LAST))
                q += 1
                folds = layer + 1 < DEPTH
                if folds:
                    shift_hi(2 * layer + 2)
                after = 0 if layer + 1 == DEPTH else 2 if KIND[layer + 1] == "pool" else KD
                out_quad(q, 0, 2 * layer + 2, (LAST,) * 4, True, folds)
                out_quad(q + 1, 4, 2 * layer + 2, (LAST, LAST, after, after), True, folds)
            rms_of(2 * DEPTH)

        @block.vector
        def _(dve):
            def split_lo(q, j, tiles):
                dve.wait_ge(w_hi_ready, 4 * q + (j + 1))
                dve.tensor_tensor(w_lo[:, j % 2, 0:tiles * P], raw[:, j, 0:tiles * P],
                                  w_hi[:, j % 2, 0:tiles * P].bitcast(F32), ALU.subtract).then_inc(w_lo_ready, 1)

            def step(q, j, tiles):
                if tiles:
                    split_lo(q + (j + 2) // 4, (j + 2) % 4, tiles)
                dve.wait_ge(unit_done, 4 * q + (j + 1))

            def evacuated(q, j):
                return 2 * q + (j // 2 + 2)

            def g_lo_of(src, index, count):
                dve.wait_ge(g_hi_ready, count)
                dve.tensor_tensor(g_lo[:, index, :], src, g_hi[:, index, :].bitcast(F32), ALU.subtract).then_inc(g_ready, 1)
                dve.wait_ge(g_ready, count)

            def ada_sum(qa, j, v, first=False):
                if j == 0 and v == 0 and not first:
                    dve.wait_ge(ada_kept, qa)
                if v == 0:
                    dve.wait_ge(ada_in[j], 16 * qa + 16)
                if not first or j or v:
                    dve.wait_ge(ada_step, 2 * ADA_N * qa + (2 * j + v))
                dve.tensor_tensor_reduce(ada_products, ada_w[:, j * D:(j + 1) * D], cond[:, v, :], 1.0, 0.0,
                                         ALU.mult, ALU.add, ada_raw[:, j, v:v + 1]).then_inc(ada_step, 1)

            def keep_ada(qa):
                dve.wait_ge(ada_step, 2 * ADA_N * qa + 2 * ADA_N)
                dve.tensor_tensor(mod[:, bass.ds(ADA_N * qa + ADA_PE, ADA_N), :], ada_raw[:],
                                  mod[:, bass.ds(ADA_N * qa + ADA_PE, ADA_N), :], ALU.add).then_inc(ada_kept, 1)

            def ada_share(qa, begin, end):
                for e in range(begin, end):
                    n, v = e // 2, e % 2
                    ada_sum(qa + n // ADA_N, n % ADA_N, v)
                    if n % ADA_N == ADA_N - 1 and v:
                        keep_ada(qa + n // ADA_N)

            def ada_in_step(qa, j):
                if qa is not None:
                    ada_share(qa, (0, 2, 3, 5)[j], (2, 3, 5, 6)[j])

            def ada_twice(qa, j):
                if qa is not None:
                    ada_share(qa, 3 * j, 3 * j + 3)

            def ada_triple(qa):
                ada_share(qa, 0, 2 * ADA_N)

            def gain_of(layer, which):
                dve.wait_ge(ada_kept, (ADA_HEAD, ADA_HEAD + Q_ZU + 2 * Q_B)[which] if layer == 0 else ADA_Q * (layer + 1) - ADA_PE // ADA_N)
                at = ADA_T * layer + KD * (SCALE1, SCALE2)[which]
                o = KD * (2 * layer + which)
                dve.scalar_tensor_tensor(out=gain[:, o:o + KD, :], in0=mod[:, at:at + KD, :], scalar=1.0,
                                         in1=gain[:, o:o + KD, :], op0=ALU.add, op1=ALU.mult).then_inc(gain_ready, 1)

            def scaled_out(q, j, row, off_s=0, off_p=TS):
                slot = j % 2
                dve.tensor_copy(bias[:, j, :], ps[:, 2 * slot + 1, T - TA:TH - TA])
                for (src, dst), (_, r) in zip(parts(slot, row, off_s, off_p), parts(slot, rinv)):
                    v = dve.tensor_tensor(dst, src, r, ALU.mult)
                v.then_inc(freed[slot], 1)
                dve.wait_ge(freed[slot], evacuated(q, j))

            def times(j, row, other, off_s=0, off_p=TS, other_s=0, other_p=TS):
                for g, (at, o, n) in enumerate(((off_s, other_s, TS), (off_p, other_p, TP))):
                    v = dve.scalar_tensor_tensor(out=row[:, at:at + n], in0=row[:, at:at + n], scalar=bias[:, j, g:g + 1],
                                                 in1=other[:, o:o + n], op0=ALU.add, op1=ALU.mult)
                v.then_inc(product_ready, 1)

            def ffn_in_quad(q, i, count, pairs, products, ada=None, tiles=(KD,) * 4):
                for j in range(4):
                    step(q, j, tiles[j])
                    pair = j // 2
                    if j % 2 == 0:
                        scaled_out(q, j, pair_a[:, pair, :])
                    else:
                        scaled_out(q, j, pair_b[:, pair, :])
                        dve.wait_ge(gate_ready, pairs + (pair + 1))
                        times(j, pair_b[:, pair, :], pair_a[:, pair, :])
                        index = slice(2 * i + pair, 2 * i + pair + 1) if isinstance(i, int) else bass.ds(2 * i + pair, 1)
                        g_lo_of(pair_b[:, pair:pair + 1, :], index, count + (pair + 1))
                    ada_in_step(ada, j)

            def out_quad(q, m0, n, gate, tiles, squares, folds=True, ada=None, triples=1):
                for j in range(4):
                    m = m0 + j
                    late = squares and m == KD - 1
                    if not late:
                        step(q, j, tiles[j])
                    else:
                        dve.wait_ge(unit_done, 4 * q + (j + 1))
                    for g, (src, dst) in enumerate(parts(j % 2, x[:, m, :]) if isinstance(m0, int) else
                                                   dynamic_parts(j % 2, m)):
                        v = dve.scalar_tensor_tensor(out=dst, in0=src, scalar=gate(m, g), in1=dst,
                                                     op0=ALU.mult, op1=ALU.add)
                    v.then_inc(freed[j % 2], 1)
                    if squares:
                        if folds:
                            dve.wait_ge(freed[j % 2], evacuated(q, j))
                        if m >= 2:
                            add_square(m - 1, n)
                        if late:
                            add_square(m, n)
                        if folds:
                            fold_lo(m, n)
                    if late:
                        step(q, j, tiles[j])
                    if triples == 1:
                        ada_in_step(ada, j)
                    else:
                        ada_twice(ada, j)

            def fold_lo(m, n):
                dve.wait_ge(h_hi_ready, H_BASE[n] + m + 1)
                for g, (lo, hi) in enumerate(((0, TS), (TS, T))):
                    v = dve.scalar_tensor_tensor(out=h_lo[:, m, lo:hi], in0=x[:, m, lo:hi], scalar=gain[:, KD * n + m, g:g + 1],
                                                 in1=h_hi[:, m, lo:hi].bitcast(F32), op0=ALU.mult, op1=ALU.subtract)
                v.then_inc(h_ready, 1)

            def shift_lo(n):
                dve.wait_ge(shift_hi_ready, H_BASE[n] // KD + 1)
                at = ADA_T * (n // 2) + KD * (SHIFT1, SHIFT2)[n % 2]
                dve.tensor_tensor(h_lo[:, :, T:TH], mod[:, at:at + KD, :], h_hi[:, :, T:TH].bitcast(F32),
                                  ALU.subtract).then_inc(shift_ready, 1)

            def dynamic_parts(slot, m):
                row = x[:, bass.ds(m, 1), :].rearrange("p a t -> p (a t)")
                return parts(slot, row)

            def add_square(m, n):
                dve.wait_ge(sq_ready, KD * n + m + 1)
                if m >= 2:
                    dve.wait_ge(sq_added, (KD - 1) * n + m - 1)
                dve.tensor_tensor(sq_sum, sq_sum, sq[:, m % 2, :], ALU.add).then_inc(sq_added, 1)

            def gate_of(block_):
                def gate(m, g):
                    at = ADA_T * layer + KD * block_
                    if isinstance(m, int):
                        return mod[:, at + m, g:g + 1]
                    return mod[:, bass.ds(m + at, 1), g:g + 1].rearrange("p a b -> p (a b)")
                return gate

            def inverse_rms(n):
                dve.wait_ge(rms_ready, n + 1)
                dve.reciprocal(rinv, rms).then_inc(rinv_ready, 1)
                dve.wait_ge(rinv_ready, n + 1)

            def conv(layer, q, g):
                ada = layer == 0
                jc = layer // 3
                z = tmp[:, 4:6, 0:CW]
                for at in (0, CS + TS, CP - 1, CW - 1):
                    dve.memset(z[:, :, at:at + 1], 0.0)
                dve.memset(marks[:, 3:4], 0.0).then_inc(pads_ready, 1)
                dve.wait_ge(pads_ready, jc + 1 + (1 if layer > 1 else 0))
                if layer:
                    dve.wait_ge(kv_stored, 32)
                with dve.Fori(0, Q_ZU) as i:
                    for j in range(4):
                        step(i + q, j, KD)
                        pair = j // 2
                        if j % 2 == 0:
                            scaled_out(i + q, j, pair_a[:, pair, :])
                        else:
                            row = z[:, pair, :]
                            scaled_out(i + q, j, row, CS, CP)
                            dve.wait_ge(gate_ready, 2 * i + (LAYER_P[layer] + pair + 1))
                            times(j, row, pair_a[:, pair, :], off_s=CS, off_p=CP)
                            dve.wait_ge(product_ready, 2 * i + (LAYER_R[layer] + pair + 1))
                            out = mix[:, bass.ds(i * (2 * CW) + (pair * CW + 1), CW - 2)]
                            for n, tap in enumerate((1, 0, 2)):
                                w = conv_w[:, bass.ds(2 * i + ((jc * 3 + tap) * KD + pair), 1)]
                                if n == 0:
                                    v = dve.tensor_scalar(out, row[:, 1:CW - 1], w, None, ALU.mult)
                                else:
                                    dve.wait_ge(conv_step, 6 * i + (jc * 3 * KD + 3 * pair + n))
                                    v = dve.scalar_tensor_tensor(out=out, in0=row[:, tap:tap + CW - 2], scalar=w,
                                                                 in1=out, op0=ALU.mult, op1=ALU.add)
                                v.then_inc(conv_step, 1)
                            dve.wait_ge(conv_step, 6 * i + (jc * 3 * KD + 3 * pair + 3))
                        ada_in_step(i + ADA_HEAD if ada else None, j)
                q += Q_ZU
                dve.wait_ge(conv_step, (jc + 1) * 3 * KD)
                with dve.Fori(0, Q_B) as i:
                    for j in range(4):
                        step(i + q, j, KD)
                        row = mix[:, bass.ds(i * (4 * CW) + j * CW, CW)]
                        scaled_out(i + q, j, pair_b[:, j % 2, :])
                        times(j, pair_b[:, j % 2, :], row, other_s=CS, other_p=CP)
                        if ada:
                            ada_share(2 * i + (ADA_HEAD + Q_ZU), 3 * j, 3 * j + 1)
                        g_lo_of(pair_b[:, j % 2:j % 2 + 1, :], bass.ds(4 * i + j, 1), 4 * i + (g + j + 1))
                        if ada:
                            ada_share(2 * i + (ADA_HEAD + Q_ZU), 3 * j + 1, 3 * j + 3)
                q += Q_B
                if ada:
                    gain_of(layer, 1)
                shift_lo(2 * layer + 1)
                for half in range(Q_OUT):
                    out_quad(q + half, 4 * half, 2 * layer + 1, gate_of(GATE1), (KD,) * 4, True,
                             ada=ADA_HEAD + Q_ZU + 2 * Q_B + half if ada else None)

            def pooling(layer, q):
                steps = [0]
                n = 2 * layer + 1

                def chained(ins):
                    ins.then_inc(pool_step, 1)
                    steps[0] += 1
                    dve.wait_ge(pool_step, steps[0])

                def scale(group):
                    for m in (2 * group, 2 * group + 1):
                        if m < KD - 1:
                            step(q + m // 4, m % 4, 2 if m < KD - 2 else KD)
                        else:
                            dve.wait_ge(unit_done, 4 * q + KD)
                        scaled_out(q + m // 4, m % 4, pool_rows[:, m % 4, :], PS0, PP0)

                def pool_group(group):
                    rows = pool_rows[:, group % 2 * 2:group % 2 * 2 + 2, :]
                    dve.wait_ge(row_ready, 2 * group + 2)
                    lo, hi = 1, PW
                    chained(dve.tensor_tensor(window_a[:, :, lo:hi], rows[:, :, lo - 1:hi - 1], rows[:, :, lo:hi], ALU.add))
                    src, other = window_a, window_b
                    size = 2
                    while size < WINDOWS[group]:
                        s = size // 2
                        lo, hi = lo + s, hi - s
                        chained(dve.tensor_tensor(other[:, :, lo:hi], src[:, :, lo - s:hi - s], src[:, :, lo + s:hi + s], ALU.add))
                        src, other = other, src
                        size *= 2
                    for r in range(2):
                        blocks = src[:, r, :].rearrange("p (b e) -> p b e", e=HP)
                        for e, (at, length) in enumerate(((PS0, TS), (PP0, TP))):
                            first, last = at // HP, (at + length) // HP - 1
                            ends = blocks[:, first:last + 1:last - first, :]
                            v = dve.tensor_tensor(ends, ends, edge[:, group, 2 * e * HP:2 * (e + 1) * HP].rearrange("p (b e) -> p b e", e=HP), ALU.mult)
                    chained(v)
                    for at, lo_, n_ in ((PS0, 0, TS), (PP0, TS, TP)):
                        v = dve.scalar_tensor_tensor(out=pair_b[:, :, lo_:lo_ + n_], in0=src[:, :, at:at + n_], scalar=1.0 / WINDOWS[group],
                                                     in1=rows[:, :, at:at + n_], op0=ALU.mult, op1=ALU.subtract)
                    chained(v)
                    for r in range(2):
                        m = 2 * group + r
                        for g, (lo_, hi_) in enumerate(((0, TS), (TS, T))):
                            v = dve.scalar_tensor_tensor(out=x[:, m, lo_:hi_], in0=pair_b[:, r, lo_:hi_], scalar=pool_gate[:, m, g:g + 1],
                                                         in1=x[:, m, lo_:hi_], op0=ALU.mult, op1=ALU.add)
                        v.then_inc(pooled_ready, 1)

                def fold(group):
                    dve.wait_ge(pooled_ready, 2 * group + 2)
                    for m in (2 * group, 2 * group + 1):
                        fold_lo(m, n)

                scale(0)
                for group in range(len(WINDOWS)):
                    if group + 1 < len(WINDOWS):
                        scale(group + 1)
                        if group + 2 == len(WINDOWS):
                            shift_lo(n)
                    if group:
                        fold(group - 1)
                    pool_group(group)
                fold(len(WINDOWS) - 1)
                split_lo(q + 2, 1, KD)

            def attention(layer, q, g):
                steps = [0]

                def chained(ins):
                    ins.then_inc(head_step, 1)
                    steps[0] += 1
                    dve.wait_ge(head_step, steps[0])

                def row_max(i, n):
                    width = T if n % 5 < 4 else TP
                    dve.wait_ge(score_done, 10 * i + (n + 1))
                    dve.tensor_reduce(stat[:, 0, n % 2:n % 2 + 1], ps_flat[n % 2][:, 0:width], AX.X, ALU.max).then_inc(max_done, 1)
                    dve.wait_ge(max_done, 10 * i + (n + 1))
                    dve.tensor_scalar(stat[:, 1, n % 2:n % 2 + 1], stat[:, 0, n % 2:n % 2 + 1],
                                      q_scale[:, at_(i * (2 * T // P) + n)], -1.0, ALU.mult, ALU.mult).then_inc(bias_done, 1)

                for t in range(4 * Q_QKV + 2):
                    if t < 4 * Q_QKV:
                        step(q + t // 4, t % 4, KD)
                        scaled_out(q + t // 4, t % 4, mix[:, t * T:(t + 1) * T])
                    if t - 2 >= KVH:
                        row = mix[:, (t - 2) * T:(t - 2) * T + TS]
                        dve.wait_ge(head_turned, t - 3)
                        dve.wait_ge(late_in, 32)
                        dve.tensor_tensor(turned, ps_rot, rope[:, 1, :], ALU.mult)
                        chained(dve.tensor_tensor(row, row, rope[:, 0, :], ALU.mult))
                        dve.tensor_tensor(row, row, turned, ALU.add).then_inc(head_ready, 1)
                        dve.wait_ge(head_ready, t - 3)
                    if KVH <= t - 1 < 4 * Q_QKV:
                        row = mix[:, (t - 1) * T:t * T]
                        dve.wait_ge(head_rms, t - KVH)
                        if t - 1 < 2 * KVH:
                            chained(dve.reciprocal(head_root, head_root))
                            dve.scalar_tensor_tensor(out=row, in0=row, scalar=qk_norm[:, 1:2], in1=head_root,
                                                     op0=ALU.mult, op1=ALU.mult).then_inc(head_normed, 1)
                        else:
                            inv = q_scale[:, (t - 1 - 2 * KVH) * (T // P):(t - 2 * KVH) * (T // P)]
                            chained(dve.reciprocal(inv, inv))
                            dve.tensor_scalar(inv, inv, SCALE, None, ALU.mult)
                            dve.tensor_scalar(row, row, qk_norm[:, 0:1], None, ALU.mult).then_inc(head_normed, 1)
                    if t >= 4 * Q_QKV:
                        v = t - 4 * Q_QKV
                        dve.wait_ge(v_turned, v + 1)
                        dve.tensor_copy(v_tok[:, v, :], sum_flat[:, 0:T]).then_inc(v_kept, 1)
                        if v == 0:
                            row_max(0, 0)

                def normalise(i, n):
                    width = T if n % 5 < 4 else TP
                    dve.wait_ge(exp_done, 10 * i + (n + 1))
                    dve.reciprocal(stat[:, 3, n % 2:n % 2 + 1], stat[:, 2, n % 2:n % 2 + 1]).then_inc(inv_done, 1)
                    dve.wait_ge(inv_done, 10 * i + (n + 1))
                    dve.tensor_scalar(tmp[:, n % 2, 0:width], tmp[:, n % 2, 0:width], stat[:, 3, n % 2:n % 2 + 1],
                                      None, ALU.mult).then_inc(prob_ready, 1)

                def mixed_lo(i, hh):
                    dve.wait_ge(g_hi_ready, 2 * i + (g + hh + 1))
                    at = at_(2 * i + hh)
                    dve.tensor_tensor(g_lo[:, at, 0:TS], ps_rot.rearrange("p (a n) -> p a n", a=1),
                                      g_hi[:, at, 0:TS].bitcast(F32), ALU.subtract)
                    dve.tensor_tensor(g_lo[:, at, TS:T], ps_mixed.rearrange("p (a n) -> p a n", a=1),
                                      g_hi[:, at, TS:T].bitcast(F32), ALU.subtract).then_inc(g_ready, 1)

                def pair(i, first=False, last=False):
                    for n in range(10):
                        if n + 1 < 10 or not last:
                            row_max(i, n + 1)
                        normalise(i, n)
                        if n == 2 and not first:
                            mixed_lo(i - 1, 1)
                        if n == 7:
                            mixed_lo(i, 0)

                pair(0, first=True)
                with dve.Fori(1, HEADS // 2 - 1) as i:
                    pair(i)
                pair(HEADS // 2 - 1, last=True)
                mixed_lo(HEADS // 2 - 1, 1)
                q += Q_QKV
                shift_lo(2 * layer + 1)
                for half in range(Q_OUT):
                    out_quad(q + half, 4 * half, 2 * layer + 1, gate_of(GATE1), (KD,) * 4, True)

            dve.wait_ge(cond_ready, 1)
            for j in range(ADA_N):
                for v in range(2):
                    ada_sum(0, j, v, first=True)
            dve.wait_ge(consts_in, CONSTS * 16)
            keep_ada(0)
            with dve.Fori(1, ADA_HEAD) as i:
                ada_triple(i)
            split_lo(0, 0, KD)
            split_lo(0, 1, KD)
            dve.wait_ge(head_tile, ADA_PE)
            dve.tensor_tensor(mod[:, 0:ADA_PE, :], head_out, mod[:, 0:ADA_PE, :], ALU.add).then_inc(head_kept, 1)
            dve.wait_ge(head_kept, 1)
            gain_of(0, 0)
            shift_lo(0)
            dve.wait_ge(x_in, 16 * X_PIECES)
            dve.wait_ge(gain_ready, 1)
            for m in range(KD):
                fold_lo(m, 0)
            for layer in range(DEPTH):
                q, g, kind, pr, r = LAYER_Q[layer], LAYER_G[layer], KIND[layer], LAYER_P[layer], LAYER_R[layer]
                inverse_rms(2 * layer)
                if kind == "pool":
                    dve.wait_ge(pads_ready, 2)
                    dve.wait_ge(pool_gate_ready, 1)
                    pooling(layer, q)
                else:
                    (conv if kind == "conv" else attention)(layer, q, g)
                if kind == "conv":
                    pr += KD
                    r += 2 * KD
                q += Q_MIX[kind]
                g += G_MIX[kind]
                inverse_rms(2 * layer + 1)
                ada = layer + 1 < DEPTH
                qa = ADA_Q * (layer + 1) - ADA_PE // ADA_N
                with dve.Fori(0, 2) as c:
                    with dve.Fori(0, Q_IN) as i:
                        ffn_in_quad(c * (Q_IN + Q_OUT) + i + q, i, c * CHUNK + 2 * i + g, c * CHUNK + 2 * i + pr,
                                    c * CHUNK + 2 * i + r, ada=c * (Q_IN + 2 * Q_OUT) + i + qa if ada else None)
                    with dve.Fori(0, Q_OUT) as i:
                        out_quad(c * (Q_IN + Q_OUT) + i + (q + Q_IN), 4 * i, 0, gate_of(GATE2), (KD,) * 4, False,
                                 ada=c * (Q_IN + 2 * Q_OUT) + 2 * i + (qa + Q_IN) if ada else None, triples=2)
                if ada:
                    gain_of(layer + 1, 0)
                    gain_of(layer + 1, 1)
                    if KIND[layer + 1] == "pool":
                        for a, b in ((0, PS0), (PS0 + TS, PP0), (PP0 + TP, PW)):
                            dve.memset(pool_rows[:, :, a:b], 0.0)
                        dve.memset(marks[:, 3:4], 0.0).then_inc(pads_ready, 1)
                        at = ADA_T * (layer + 1) + KD * GATE1
                        dve.tensor_tensor(pool_gate[:], pool_s[:], mod[:, at:at + KD, :], ALU.mult).then_inc(pool_gate_ready, 1)
                q += 2 * (Q_IN + Q_OUT)
                g += 2 * CHUNK
                pr += 2 * CHUNK
                r += 2 * CHUNK
                with dve.Fori(0, Q_LAST - 1) as i:
                    ffn_in_quad(i + q, i, 2 * i + g, 2 * i + pr, 2 * i + r)
                q += Q_LAST - 1
                last = 2 * (Q_LAST - 1)
                ffn_in_quad(q, Q_LAST - 1, g + last, pr + last, r + last, tiles=(KD, KD, LAST, LAST))
                q += 1
                folds = ada
                if folds:
                    shift_lo(2 * layer + 2)
                after = 0 if layer + 1 == DEPTH else 2 if KIND[layer + 1] == "pool" else KD
                out_quad(q, 0, 2 * layer + 2, gate_of(GATE2), (LAST,) * 4, True, folds)
                out_quad(q + 1, 4, 2 * layer + 2, gate_of(GATE2), (LAST, LAST, after, after), True, folds)
            inverse_rms(2 * DEPTH)
            for k in range(KD):
                dve.scalar_tensor_tensor(out=mix[:, k * T:(k + 1) * T], in0=x[:, k, :], scalar=final_w[:, k:k + 1],
                                         in1=rinv, op0=ALU.mult, op1=ALU.mult).then_inc(y_ready, 1)


def _units(w, order):
    k, n = w.shape
    u = w.reshape(k // P, P, n // P, P).transpose(2, 1, 0, 3)[order].reshape(len(order), P, k)
    if k < KD * P:
        u = np.concatenate([u, np.zeros((len(order), P, KD * P - k), w.dtype)], axis=2)
    return u


def _rows(v):
    return np.moveaxis(v.reshape(*v.shape[:-1], -1, P), -1, 0)


def _twice(v):
    return np.repeat(v[..., None], 2, axis=-1)


def _rope():
    axis = P // 2
    inv = 10000.0 ** (-np.arange(0, axis, 2, dtype=np.float32) / np.float32(axis))
    t = np.arange(TS)
    out = np.zeros((P, 2, TS), np.float32)
    for a, pos in enumerate((t // GRID_W, t % GRID_W)):
        ang = (pos[None, :].astype(np.float32) * inv[:, None].astype(np.float32)).astype(np.float32)
        for half in range(2):
            at = a * axis + half * (axis // 2)
            out[at:at + axis // 2, 0] = np.cos(ang)
            out[at:at + axis // 2, 1] = np.sin(ang)
    return out


def _turn():
    m = np.zeros((P, P), np.float32)
    for a in range(0, P, 64):
        for i in range(32):
            m[a + 32 + i, a + i] = -1.0
            m[a + i, a + 32 + i] = 1.0
    return m


def _edge():
    out = np.ones((P, len(WINDOWS), 4 * HP), np.float32)
    for g, w in enumerate(WINDOWS):
        for n, length in enumerate((TS, TP)):
            for e, start in enumerate((0, length - HP)):
                for i in range(HP):
                    t = start + i
                    count = min(t + w // 2, length) - max(t - w // 2, 0)
                    out[:, g, (2 * n + e) * HP + i] = w / count
    return out


def kernel(**inputs):
    import concourse.bacc as _bacc
    from concourse.bass_utils import run_bass_kernel_spmd as _run

    a = {k: np.asarray(v) for k, v in inputs.items()}
    ffn_in = [np.concatenate([_units(a["ffn_in_w"][i], [n for j in range(FT) for n in (j, FT + j)])]) for i in range(DEPTH)]

    def ffn(i):
        w_out = a["ffn_out_w"][i]
        parts_ = []
        for c in range(3):
            lo, hi = CHUNK * c, min(CHUNK * (c + 1), FT)
            parts_.append(ffn_in[i][2 * lo:2 * hi])
            parts_.append(_units(w_out[lo * P:hi * P], list(range(KD))))
        return parts_

    units = []
    for i in range(DEPTH):
        j = i // 3
        if KIND[i] == "conv":
            units.append(_units(a["conv_in_w"][j], [n for m in range(KD) for n in (KD + m, 2 * KD + m)] + list(range(KD))))
            units.append(_units(a["conv_out_w"][j], list(range(KD))))
        elif KIND[i] == "pool":
            units += [_units(a["pool_w"][j, g], [0, 1]) for g in range(len(WINDOWS))]
        else:
            units.append(_units(a["attn_qkv_w"][j], [10, 11, 8, 9, *range(HEADS)]))
            units.append(_units(a["attn_out_w"][j], list(range(KD))))
        units += ffn(i)
    tokens = np.concatenate([a["x_sample"][0], a["x_prompt"][0]], axis=0)
    arrays = {
        "weights": np.concatenate(units),
        "ada_w": a["ada_w"].transpose(0, 2, 1).reshape(DEPTH * ADA_T, P, D)[ADA_PE:],
        "ada_head": _units(a["ada_w"][0], list(range(ADA_PE))),
        "x": _rows(tokens).transpose(0, 2, 1),
        "cond_k": _rows(np.stack([a["c"][0], a["c_ctx"]])).transpose(0, 2, 1),
        "cond": np.repeat(np.stack([a["c"][0], a["c_ctx"]])[None], P, axis=0),
        "ada_b": _twice(_rows(a["ada_b"]).reshape(P, -1)),
        "norm_w": _twice(_rows(np.stack([a["norm1_w"], a["norm2_w"]], axis=1)).reshape(P, -1)),
        "ident": np.eye(P, dtype=np.float32),
        "turn": _turn(),
        "conv_w": _rows(a["conv_w"]).reshape(P, -1),
        "qk_norm": np.stack([a["q_norm_w"][0], a["k_norm_w"][0]], axis=-1),
        "final_w": _rows(a["final_norm_w"]),
        "edge": _edge(),
        "pool_s": _twice(_rows(a["pool_scale"][0])),
        "rope": _rope(),
        "cache_k": a["cache_k"][0, 0].transpose(2, 0, 1),
        "cache_v": a["cache_v"][0, 0].transpose(1, 0, 2),
    }
    outs = {"y": (P, KD, T), "new_k": (P, KVH, TP), "new_v": (P, KVH, TP)}
    nc = _bacc.Bacc("TRN2", target_bir_lowering=False, num_devices=1)
    d, feed = {}, {}
    for name, v in arrays.items():
        v = np.ascontiguousarray(v)
        feed["in_" + name] = v
        d[name] = nc.dram_tensor("in_" + name, v.shape, mybir.dt.from_np(v.dtype), kind="ExternalInput").ap()
    for name, shape in outs.items():
        d[name] = nc.dram_tensor("out_" + name, shape, F32, kind="ExternalOutput").ap()
    build(nc, d)
    r = _run(nc, [feed], core_ids=[0]).results[0]
    y = r["out_y"].transpose(2, 1, 0).reshape(T, D)
    new_k = r["out_new_k"].transpose(1, 2, 0)[None, None]
    new_v = r["out_new_v"].transpose(1, 2, 0)[None, None]
    return (np.ascontiguousarray(y[TS:][None]), np.ascontiguousarray(y[:TS][None]),
            np.ascontiguousarray(new_k), np.ascontiguousarray(new_v))
```
